# Optimizing a Trainium2 kernel written in Bass

```python
import math
import jax, jax.numpy as jnp
from jax import lax
import numpy as np

D_MODEL = 1024
BATCH = 1
SEQ = 512
DEPTH = 1

MLA_HEADS = 8
MLA_NOPE = 64
MLA_ROPE = 32
MLA_V = 64
Q_LORA = 384
KV_LORA = 256
ROPE_THETA = 10000.0
MLA_QK = MLA_NOPE + MLA_ROPE
MLA_WIDTH = MLA_HEADS * MLA_V

DIL_HEADS = 8
DIL_HEAD_DIM = 64
DIL_PATTERNS = ((128, 1), (512, 4), (2048, 16))
DIL_WIDTH = DIL_HEADS * DIL_HEAD_DIM

BLOCK = 128
N_BRANCH = 2
D_FF = 4 * D_MODEL
LN_EPS = 1e-5
RMS_EPS = 1e-6
NEG = -1e30
ALPHA = (2 * DEPTH) ** 0.25
BETA = (8 * DEPTH) ** -0.25

SPLITS = (Q_LORA,
          Q_LORA + KV_LORA,
          Q_LORA + KV_LORA + MLA_ROPE,
          Q_LORA + KV_LORA + MLA_ROPE + 3 * DIL_WIDTH)
IN_WIDTH = Q_LORA + KV_LORA + MLA_ROPE + 3 * DIL_WIDTH + N_BRANCH * D_MODEL

kernel_name = 'hybrid_mla_dilated_gated_deepnorm'

def layer_norm(x, g, b):
    xf = x.astype(jnp.float32)
    mu = jnp.mean(xf, axis=-1, keepdims=True)
    var = jnp.mean(jnp.square(xf - mu), axis=-1, keepdims=True)
    y = (xf - mu) * lax.rsqrt(var + LN_EPS) * g.astype(jnp.float32) + b.astype(jnp.float32)
    return y.astype(x.dtype)

def rms_norm(x, g):
    xf = x.astype(jnp.float32)
    y = xf * lax.rsqrt(jnp.mean(jnp.square(xf), axis=-1, keepdims=True) + RMS_EPS)
    return (y * g.astype(jnp.float32)).astype(x.dtype)

def apply_rope(t, pos):
    half = t.shape[-1] // 2
    inv = jnp.power(ROPE_THETA, -jnp.arange(half, dtype=jnp.float32) / half)
    ang = pos.astype(jnp.float32)[:, None] * inv[None, :]
    cos = jnp.cos(ang)[None, :, None, :]
    sin = jnp.sin(ang)[None, :, None, :]
    tf = t.astype(jnp.float32)
    t1, t2 = tf[..., :half], tf[..., half:]
    return jnp.concatenate([t1 * cos - t2 * sin, t1 * sin + t2 * cos], axis=-1).astype(t.dtype)

def alibi_slopes(n):
    return jnp.asarray([2.0 ** (-8.0 * (i + 1) / n) for i in range(n)], dtype=jnp.float32)

def mla_attention(q_a, kv_a, k_r, g_q_a, w_uq, g_kv_a, w_ukv):
    B, S, _ = q_a.shape
    pos = jnp.arange(S)
    q = (rms_norm(q_a, g_q_a) @ w_uq).reshape(B, S, MLA_HEADS, MLA_QK)
    q = jnp.concatenate([q[..., :MLA_NOPE], apply_rope(q[..., MLA_NOPE:], pos)], axis=-1)
    kv = (rms_norm(kv_a, g_kv_a) @ w_ukv).reshape(B, S, MLA_HEADS, MLA_NOPE + MLA_V)
    k_rope = apply_rope(k_r[:, :, None, :], pos)
    k = jnp.concatenate([kv[..., :MLA_NOPE],
                         jnp.broadcast_to(k_rope, (B, S, MLA_HEADS, MLA_ROPE))], axis=-1)
    v = kv[..., MLA_NOPE:]
    scale = MLA_QK ** -0.5
    nb = S // BLOCK
    q_blocks = q.reshape(B, nb, BLOCK, MLA_HEADS, MLA_QK).transpose(1, 0, 2, 3, 4)
    kpos = jnp.arange(S)

    def one_block(args):
        qb, i = args
        s = jnp.einsum('bqhd,bkhd->bhqk', qb, k).astype(jnp.float32) * scale
        qpos = i * BLOCK + jnp.arange(BLOCK)
        s = jnp.where((kpos[None, :] <= qpos[:, None])[None, None], s, NEG)
        p = jax.nn.softmax(s, axis=-1).astype(v.dtype)
        return jnp.einsum('bhqk,bkhd->bqhd', p, v)

    o = lax.map(one_block, (q_blocks, jnp.arange(nb)))
    return o.transpose(1, 0, 2, 3, 4).reshape(B, S, MLA_WIDTH)

def dilated_pattern(q, k, v, window, dilation, slopes):
    B, S, H, Dh = q.shape
    L = S // dilation
    J = window // dilation
    C = min(BLOCK, L)
    nb = -(-L // C)
    Lp = nb * C

    def to_classes(t):
        t = t.reshape(B, L, dilation, H, Dh).transpose(0, 2, 1, 3, 4)
        t = jnp.pad(t, ((0, 0), (0, 0), (0, Lp - L), (0, 0), (0, 0)))
        return t.reshape(B, dilation, nb, C, H, Dh)

    def with_prev(t):
        prev = jnp.pad(t, ((0, 0), (0, 0), (1, 0), (0, 0), (0, 0), (0, 0)))[:, :, :-1]
        return jnp.concatenate([prev, t], axis=3)

    def from_classes(t):
        X = t.shape[-1]
        t = t.reshape(B, dilation, Lp, H, X)[:, :, :L]
        return t.transpose(0, 2, 1, 3, 4).reshape(B, S, H, X)

    qc = to_classes(q)
    kc = with_prev(to_classes(k))
    vc = with_prev(to_classes(v))
    s = jnp.einsum('brnqhd,brnkhd->brnhqk', qc, kc).astype(jnp.float32) * (Dh ** -0.5)
    qi = jnp.arange(C)[:, None] + C
    ki = jnp.arange(2 * C)[None, :]
    dist = qi - ki
    valid = (dist >= 0) & (dist <= J)
    key_exists = (jnp.arange(nb)[:, None] > 0) | (jnp.arange(2 * C)[None, :] >= C)
    mask = valid[None] & key_exists[:, None, :]
    bias = -slopes[:, None, None] * (dilation * dist).astype(jnp.float32)[None]
    s = jnp.where(mask[None, None, :, None], s + bias, NEG)
    m = jnp.max(s, axis=-1)
    p = jnp.exp(s - m[..., None])
    den = jnp.sum(p, axis=-1)
    o = jnp.einsum('brnhqk,brnkhd->brnqhd', p, vc.astype(jnp.float32))
    den_t = den.transpose(0, 1, 2, 4, 3)[..., None]
    m_t = m.transpose(0, 1, 2, 4, 3)[..., None]
    return from_classes(o / den_t), from_classes(m_t), from_classes(den_t)

def dilated_attention(q, k, v):
    slopes = alibi_slopes(DIL_HEADS)
    res = [dilated_pattern(q, k, v, w, d, slopes) for (w, d) in DIL_PATTERNS]
    m_all = res[0][1]
    for r in res[1:]:
        m_all = jnp.maximum(m_all, r[1])
    num = 0.0
    tot = 0.0
    for o, m, den in res:
        wgt = den * jnp.exp(m - m_all)
        num = num + wgt * o
        tot = tot + wgt
    return (num / tot).astype(q.dtype)

def hybrid_layer(x, w_in, b_gate, g_q_a, w_uq, g_kv_a, w_ukv, w_o_mla, w_o_dil,
                 w_out, ln1_g, ln1_b, w_ff1, w_ff2, ln2_g, ln2_b):
    B, S, D = x.shape
    proj = x @ w_in
    q_a, kv_a, k_r, qkv_d, gates = jnp.split(proj, SPLITS, axis=-1)
    y_a = mla_attention(q_a, kv_a, k_r, g_q_a, w_uq, g_kv_a, w_ukv) @ w_o_mla
    qkv_d = qkv_d.reshape(B, S, 3, DIL_HEADS, DIL_HEAD_DIM)
    o_b = dilated_attention(qkv_d[:, :, 0], qkv_d[:, :, 1], qkv_d[:, :, 2])
    y_b = o_b.reshape(B, S, DIL_WIDTH) @ w_o_dil
    g = jax.nn.sigmoid(gates.reshape(B, S, N_BRANCH, D) + b_gate)
    mixed = (g[:, :, 0] * y_a + g[:, :, 1] * y_b) @ w_out
    h = layer_norm(ALPHA * x + mixed, ln1_g, ln1_b)
    f = jnp.square(jax.nn.relu(h @ w_ff1)) @ w_ff2
    return layer_norm(ALPHA * h + f, ln2_g, ln2_b)

def setup_inputs(seed: int = 0) -> dict:
    key = jax.random.key(seed)
    ks = jax.random.split(key, 20)
    f32 = jnp.float32

    def nrm(k, shape, fan_in, scale=1.0):
        return jax.random.normal(k, shape, f32) * (fan_in ** -0.5) * scale

    def gain(k, shape):
        return 1.0 + 0.02 * jax.random.normal(k, shape, f32)

    def small(k, shape):
        return 0.02 * jax.random.normal(k, shape, f32)

    L_ = DEPTH
    return {
        'x': jax.random.normal(ks[0], (BATCH, SEQ, D_MODEL), f32),
        'w_in': nrm(ks[1], (L_, D_MODEL, IN_WIDTH), D_MODEL),
        'b_gate': small(ks[2], (L_, N_BRANCH, D_MODEL)),
        'g_q_a': gain(ks[3], (L_, Q_LORA)),
        'w_uq': nrm(ks[4], (L_, Q_LORA, MLA_HEADS * MLA_QK), Q_LORA),
        'g_kv_a': gain(ks[5], (L_, KV_LORA)),
        'w_ukv': nrm(ks[6], (L_, KV_LORA, MLA_HEADS * (MLA_NOPE + MLA_V)), KV_LORA),
        'w_o_mla': nrm(ks[7], (L_, MLA_WIDTH, D_MODEL), MLA_WIDTH, BETA),
        'w_o_dil': nrm(ks[8], (L_, DIL_WIDTH, D_MODEL), DIL_WIDTH, BETA),
        'w_out': nrm(ks[9], (L_, D_MODEL, D_MODEL), D_MODEL, BETA),
        'ln1_g': gain(ks[10], (L_, D_MODEL)),
        'ln1_b': small(ks[11], (L_, D_MODEL)),
        'w_ff1': nrm(ks[12], (L_, D_MODEL, D_FF), D_MODEL, BETA),
        'w_ff2': nrm(ks[13], (L_, D_FF, D_MODEL), D_FF, BETA),
        'ln2_g': gain(ks[14], (L_, D_MODEL)),
        'ln2_b': small(ks[15], (L_, D_MODEL)),
    }

def reference(x, w_in, b_gate, g_q_a, w_uq, g_kv_a, w_ukv, w_o_mla, w_o_dil,
              w_out, ln1_g, ln1_b, w_ff1, w_ff2, ln2_g, ln2_b):
    for l in range(DEPTH):
        x = hybrid_layer(x, w_in[l], b_gate[l], g_q_a[l], w_uq[l], g_kv_a[l], w_ukv[l],
                         w_o_mla[l], w_o_dil[l], w_out[l], ln1_g[l], ln1_b[l],
                         w_ff1[l], w_ff2[l], ln2_g[l], ln2_b[l])
    return x


_drawn_inputs = setup_inputs


def setup_inputs(seed=0):
    import zlib

    import numpy as np

    out = dict(_drawn_inputs(seed))
    spreads = {}
    factors = {'b_gate': 8.0,
     'g_q_a': 8.0,
     'w_uq': 2.756,
     'g_kv_a': 8.0,
     'ln1_g': 8.055,
     'ln1_b': 7.835,
     'ln2_g': 8.24,
     'ln2_b': 8.232}
    for name, (base, spread) in spreads.items():
        noise = np.random.default_rng([zlib.crc32(name.encode()), seed]).standard_normal(out[name].shape)
        drawn = base * np.exp(spread * noise) if base else spread * noise
        out[name] = __import__('jax').numpy.asarray(drawn.astype(out[name].dtype))
    for name, factor in factors.items():
        out[name] = (out[name] * factor).astype(out[name].dtype)
    return out
```

```python
import numpy as np

import concourse.bass as bass
from concourse import mybir
from contextlib import ExitStack

F32 = mybir.dt.float32
F32R = mybir.dt.float32r
ALU = mybir.AluOpType
ACT = mybir.ActivationFunctionType
AX = mybir.AxisListType

D, S, DFF = 1024, 512, 4096
P = 128
NT = S // P
KD = D // P
KF = DFF // P
HEADS, NOPE, ROPE, VD = 8, 64, 32, 64
QK = NOPE + ROPE
HALF = ROPE // 2
QL, KVL = 384, 256
NQL, NKVL = QL // P, KVL // P
NLORA = NQL + NKVL
DW = HEADS * 64
C_DIL = QL + KVL + ROPE
C_GATE = C_DIL + 3 * DW
LN_EPS, RMS_EPS = 1e-5, 1e-6
NEG = -1e30
ALPHA = 2.0 ** 0.25
MLA_SCALE = QK ** -0.5
DIL_SCALE = 64 ** -0.5
SLOPES = [2.0 ** (-8.0 * (i + 1) / HEADS) for i in range(HEADS)]
PATTERNS = ((128, 1), (512, 4), (2048, 16))

K_ID, K_CAUSAL, K_COS, K_SIN, K_DIST, K_COUNT = 0, P, 2 * P, 2 * P + NT * HALF, 2 * P + 2 * NT * HALF, 2 * P + 2 * NT * HALF + S
K_ALL = K_COUNT + S
SMALL = K_DIST


def constants():
    t = np.zeros((P, K_ALL), np.float32)
    t[:, K_ID:K_ID + P] = np.eye(P)
    row, col = np.arange(P)[:, None], np.arange(P)[None, :]
    t[:, K_CAUSAL:K_CAUSAL + P] = np.where(col <= row, 0.0, NEG)
    inv = np.power(np.float32(10000.0), -np.arange(HALF, dtype=np.float32) / np.float32(HALF)).astype(np.float32)
    pos = (np.arange(NT)[None, :] * P + np.arange(P)[:, None]).astype(np.float32)
    ang = (pos[:, :, None] * inv[None, None, :]).astype(np.float32)
    t[:, K_COS:K_COS + NT * HALF] = np.cos(ang).reshape(P, -1)
    t[:, K_SIN:K_SIN + NT * HALF] = np.sin(ang).reshape(P, -1)
    dist = (S - P) + np.arange(P)[:, None] - np.arange(S)[None, :]
    count = np.zeros((P, S))
    for window, dilation in PATTERNS:
        count += (dist >= 0) & (dist % dilation == 0) & (dist <= window)
    t[:, K_DIST:K_DIST + S] = -dist
    t[:, K_COUNT:K_COUNT + S] = np.where(count > 0, np.log(np.maximum(count, 1)), NEG)
    return t


NPROJ = 3 * (DW // P) + 2 * KD
PRE = 1
UNITS = [("lora", m) for m in range(3)]
for _k in range(NQL):
    UNITS += [("lora", _k + 3), ("uq", _k)]
UNITS += [("proj", p) for p in range(3)] + [("ukv", k) for k in range(NKVL)] + [("proj", p) for p in range(3, NPROJ)]
UNITS += [("y", 0), ("y", 1), ("y", 2)]
for _m in range(5):
    UNITS += [("y", _m + 3), ("out", _m)]
UNITS += [("out", _m) for _m in range(5, KD)]
UNITS += [("ff1", m) for m in range(KF)] + [("ff2", 0), ("ff2", 1), ("ff2", 2)]
LAST = 8
for _k in range(KF - LAST):
    if _k + 3 < KF - LAST:
        UNITS += [("ff2", _k + 3)]
    if _k % 3 == 2:
        UNITS += [("ff2", KF - LAST + _k // 3)]
POS = {u: n for n, u in enumerate(UNITS)}
IN_RING = [u for u in UNITS if not (u[0] in ("uq", "ukv", "out") or (u[0] == "ff2" and u[1] >= KF - LAST))]
RING = {u: n for n, u in enumerate(IN_RING)}
NRAW = NRING = 3
WIDTH = {u: (HEADS * QK if u[0] == "uq" else 1024) for u in UNITS}
RAW_COUNT = {}
_count = [0] * NRAW
for _n, _u in enumerate(UNITS):
    _count[_n % NRAW] += 32 if _u[0] == "y" else 16
    RAW_COUNT[_u] = _count[_n % NRAW]

TEVENTS = [("q", 0), ("k", 0)]
for _g in range(2 * HEADS):
    if _g + 1 < HEADS:
        TEVENTS += [("q", _g + 1), ("k", _g + 1)]
    if _g >= HEADS and _g % 2 == 0:
        TEVENTS += [("v", _g)]
    TEVENTS += [("p0", _g), ("p1", _g), ("p2", _g)]
TBANK = {"q": 0, "k": 1, "v": 1, "p0": 0, "p1": 1, "p2": 0}
TI = {e: n for n, e in enumerate(TEVENTS)}
TPREV = {}
_lastof = {0: None, 1: None}
for _e in TEVENTS:
    TPREV[_e] = _lastof[TBANK[_e[0]]]
    _lastof[TBANK[_e[0]]] = TI[_e]

SPLACE = {3: (0, 0), 2: (1, 0), 1: (2, 0), 0: (2, 256)}
SORDER = [(0, (3,)), (1, (2,)), (2, (1, 0))]
POFF = {0: 0, 1: 128, 2: 384, 3: 768}
KOFF = {0: 0, 1: 512, 2: 896, 3: 1152}
PW = 1280


def layer_kernel(nc, a, out):
    st, sx, sb_, sc_ = ExitStack(), ExitStack(), ExitStack(), ExitStack()
    with st:
        def sb(name, shape, dt=F32, stack=st):
            return stack.enter_context(nc.sbuf_tensor(name, shape, dt))

        def sem(name):
            return st.enter_context(nc.semaphore(name))

        ring_h = sb("ring_high", [P, NRING, 1024], F32R)
        ring_l = sb("ring_low", [P, NRING, 1024], F32R)
        raw = sb("raw_weights", [P, NRAW, 1024])
        tab = sb("tables", [P, 2048])
        small = sb("small_constants", [P, SMALL])
        ones = sb("ones", [P, P], F32R)
        krot = sb("k_rotary", [P, NT, ROPE])
        gq = sb("g_lora", [P, NLORA])
        bg = sb("b_gate_columns", [P, 2 * KD])
        epss = sb("eps", [P, 2])
        mx = sb("row_max", [P, NT])
        nm = sb("minus_max", [P, NT])
        rs = sb("row_sum", [P, NT])
        rr = sb("row_sum_inverse", [P, NT])
        bns = sb("bn_statistics", [P, NT, 2, 6])
        mv = sb("mean_variance", [P, NT, 2])
        std = sb("deviation", [P, NT])
        rstd = sb("deviation_inverse", [P, NT])

        xt = sb("x_transposed", [P, KD, 2, S], F32R, sx)
        ot = sb("o_transposed", [P, HEADS, 2, S], F32R, sb_)
        att = sb("attention_buffers", [P, 8192], F32R, sb_)
        tok = sb("token_major", [P, 8192], F32, sb_)
        dilf = sb("dilated_qkv", [P, 3, 4, S], F32, sc_)
        pbuf = sb("probabilities", [P, 2048], F32, sc_)
        sc_.close()
        mixed = sb("mixed_transposed", [P, KD, 2, S], F32R, sb_)
        sb_.close()
        sx.close()
        tail = sb("h_residual", [P, 2, 4096])
        ff = sb("hidden_transposed", [P, KF, 2, S], F32R)

        bank = [st.enter_context(nc.psum_tensor(f"bank{n}", [P, 512], F32)) for n in range(8)]
        SB, TB, OB = bank[2:5], bank[5:7], bank[7]

        ident, causal = small[:, K_ID:K_ID + P], small[:, K_CAUSAL:K_CAUSAL + P]
        cos = small[:, K_COS:K_COS + NT * HALF].rearrange("p (t i) -> p t i", t=NT)
        sin = small[:, K_SIN:K_SIN + NT * HALF].rearrange("p (t i) -> p t i", t=NT)
        ptb = att[:, 0:2 * PW].rearrange("p (s n) -> p s n", s=2)
        qkb = att[:, 2560:6656].rearrange("p (b q s n) -> p b q s n", b=2, q=2, s=2)
        ukv = att[:, 2560:6656].rearrange("p (k s n) -> p k s n", k=2, s=2)
        uqb = [ot[:, 5:8, :, :].rearrange("p k s n -> p (k s n)")[:, n * 1536:(n + 1) * 1536] for n in range(2)] + [att[:, 0:1536]]
        uq = [b.rearrange("p (s n) -> p s n", s=2) for b in uqb]
        vb = att[:, 6656:8192].rearrange("p (s t n) -> p s t n", s=2, t=NT)
        lora = ot[:, 0:NLORA, :, :]
        xtok = tok[:, 0:4096].rearrange("p (t n) -> p t n", t=NT)
        hres = tok[:, 4096:8192].rearrange("p (t n) -> p t n", t=NT)
        qf = tok[:, 0:3072].rearrange("p (t h d) -> p t h d", t=NT, h=HEADS)
        kf = tok[:, 3072:6144].rearrange("p (t h d) -> p t h d", t=NT, h=HEADS)
        vf = tok[:, 6144:8192].rearrange("p (t h d) -> p t h d", t=NT, h=HEADS)
        z = tok[:, :].rearrange("p (m n) -> p m n", m=2 * KD)
        flat = dilf[:, :, :, :].rearrange("p c j n -> p (c j n)")
        lraw = flat[:, 0:NLORA * S].rearrange("p (m n) -> p m n", m=NLORA)
        krt = flat[0:ROPE, 2560:3072]
        rinv = flat[:, 3072:4096].rearrange("p (c n) -> p c n", c=2)
        ltmp = flat[:, 4096:5120].rearrange("p (c n) -> p c n", c=2)
        sqt = pbuf[:, 0:1024].rearrange("p (c n) -> p c n", c=2)
        sqh = qkb[:, :, :, :, :].rearrange("p b q s n -> p (b q) s n")
        rtmp = pbuf[:, 1024:1536].rearrange("p (a h i) -> p a h i", a=4, h=HEADS)
        wout = [xt, att[:, :].rearrange("p (k s n) -> p k s n", k=KD, s=2)]
        dist, lcount = tab[:, 0:S], tab[:, S:2 * S]
        bias = tab[:, 2 * S:4 * S].rearrange("p (b n) -> p b n", b=2)
        lng, lnb = tab[:, 0:D], tab[:, D:2 * D]
        relu = tab[:, 0:1024].rearrange("p (b n) -> p b n", b=2)
        fsq = tab[:, 1024:2048].rearrange("p (b n) -> p b n", b=2)
        h2 = tail[:, 0, :].rearrange("p (t n) -> p t n", t=NT)

        spill = nc.dram_tensor("h_spill", (S, D), F32).ap().rearrange("(t p) n -> p t n", p=P)

        raw_in = [sem(f"raw_in{n}") for n in range(NRAW)]
        x_in, const_in, small_in = [sem(f"x_in{t}") for t in range(NT)], sem("const_in"), sem("small_in")
        w_high, w_low = sem("w_high"), sem("w_low")
        unit_done = sem("unit_done")
        xt_ps, xt_high, xt_low = sem("xt_ps"), sem("xt_high"), sem("xt_low")
        acc_read = sem("acc_read")
        ones_set, vzero, eps_set = sem("ones_set"), sem("v_zeroed"), sem("eps_set")
        sq_high, sq_low, sum_ps, dev_set, inv_set = sem("sq_high"), sem("sq_low"), sem("sum_ps"), sem("dev_set"), sem("inv_set")
        norm_set, norm_high, norm_low = sem("norm_set"), sem("norm_high"), sem("norm_low")
        krt_ps, krot_set, krot_spread = sem("krt_ps"), sem("krot_set"), sem("krot_spread")
        qkv_ps, qkv_read, q_rot, ukv_done = sem("qkv_ps"), sem("qkv_read"), sem("q_rot"), sem("ukv_done")
        t_ps, t_high, t_low = sem("t_ps"), sem("t_high"), sem("t_low")
        sc_ps, max_set, exp_set, p_set = sem("scores_ps"), sem("max_set"), sem("exp_set"), sem("p_set")
        v_high, v_low, qk_high, qk_low = sem("v_high"), sem("v_low"), sem("qk_high"), sem("qk_low")
        pv_ps, o_high, o_low, bias_set = sem("pv_ps"), sem("o_high"), sem("o_low"), sem("bias_set")
        gate_set, mix_read, mix_set, mix_high, mix_low = sem("gate_set"), sem("mix_read"), sem("mix_set"), sem("mix_high"), sem("mix_low")
        out_ps, res_set, x2_in, ln_in, var_set, dev1_set = sem("out_ps"), sem("res_set"), [sem(f"x2_in{t}") for t in range(NT)], sem("ln_in"), sem("var_set"), sem("dev1_set")
        h_set, ht_ps, ht_high, ht_low, spilled = sem("h_set"), sem("ht_ps"), sem("ht_high"), sem("ht_low"), sem("spilled")
        relu_set, f_high, f_low = sem("relu_set"), sem("f_high"), sem("f_low")
        h2_in, ln2_in, ff2_ps, var2_set, dev2_set, y_set, out_done = sem("h2_in"), sem("ln2_in"), sem("ff2_ps"), sem("var2_set"), sem("dev2_set"), sem("y_set"), sem("out_done")
        dchain, pchain = sem("vector_chain"), sem("pool_chain")

        cols = lambda w: w.rearrange("(k p) n -> p k n", p=P)
        w_in, w_ff1, w_a, w_b = cols(a["w_in"][0]), cols(a["w_ff1"][0]), cols(a["w_o_mla"][0]), cols(a["w_o_dil"][0])

        def unit_source(u):
            kind, n = u
            if kind == "lora":
                return [(0, KD, w_in[:, :, n * P:(n + 1) * P])]
            if kind == "uq":
                return [(0, None, a["w_uq"][0][n * P:(n + 1) * P, :])]
            if kind == "ukv":
                return [(0, None, a["w_ukv"][0][n * P:(n + 1) * P, :])]
            if kind == "proj":
                c = C_DIL + (n % 3) * DW + (n // 3) * P if n < 12 else C_GATE + (n - 12) * P
                return [(0, KD, w_in[:, :, c:c + P])]
            if kind == "y":
                return [(0, 4, w_a[:, :, n * P:(n + 1) * P]), (512, 4, w_b[:, :, n * P:(n + 1) * P])]
            if kind == "out":
                return [(0, None, a["w_out"][0][n * P:(n + 1) * P, :])]
            if kind == "ff1":
                return [(0, KD, w_ff1[:, :, n * P:(n + 1) * P])]
            return [(0, None, a["w_ff2"][0][n * P:(n + 1) * P, :])]

        def split_dest(u):
            src = raw[:, POS[u] % NRAW, 0:WIDTH[u]]
            kind, n = u
            if kind == "uq":
                return src, uq[n][:, 0, :], uq[n][:, 1, :]
            if kind == "ukv":
                return src, ukv[:, n, 0, :], ukv[:, n, 1, :]
            if kind == "ff2" and n >= KF - LAST:
                j = n - (KF - LAST)
                return src, ff[:, 2 * j, :, :].rearrange("p s n -> p (s n)"), ff[:, 2 * j + 1, :, :].rearrange("p s n -> p (s n)")
            if kind == "out":
                return src, None, None
            slot = RING[u] % NRING
            return src, ring_h[:, slot, 0:WIDTH[u]], ring_l[:, slot, 0:WIDTH[u]]

        block = st.enter_context(nc.Block())

        @block.sync
        def _(sp):
            sp.dma_start(small[:, :], a["const"][:, 0:SMALL]).then_inc(small_in, 16)
            for t in range(NT):
                sp.dma_start(xtok[:, t, :], a["x"][0][t * P:(t + 1) * P, :]).then_inc(x_in[t], 16)
            for n, u in enumerate(UNITS):
                slot = n % NRAW
                if n >= NRAW:
                    sp.wait_ge(w_low, n - NRAW + 1)
                for first, tiles, src in unit_source(u):
                    dst = raw[:, slot, first:first + (tiles * P if tiles else WIDTH[u])]
                    if tiles:
                        dst = dst.rearrange("p (k n) -> p k n", k=tiles)
                    sp.dma_start(dst, src).then_inc(raw_in[slot], 16)
                if n == 2:
                    with nc.allow_non_contiguous_dma(reason="one small column per lora tile"):
                        sp.dma_start(gq[:, 0:NQL], a["g_q_a"][0].rearrange("(m p) -> p m", p=P)).then_inc(const_in, 16)
                        sp.dma_start(gq[:, NQL:NLORA], a["g_kv_a"][0].rearrange("(m p) -> p m", p=P)).then_inc(const_in, 16)
                        sp.dma_start(bg[:, :], a["b_gate"][0].rearrange("b (m p) -> p (b m)", p=P)).then_inc(const_in, 16)
                    sp.dma_start(tab[:, 0:2 * S], a["const"][:, K_DIST:K_ALL]).then_inc(const_in, 16)
            for t in range(NT):
                for n in range(2) if t == NT - 1 else (slice(None),):
                    half = slice(n * S, (n + 1) * S) if t == NT - 1 else n
                    sp.wait_ge(y_set, t + 1 + (n if t == NT - 1 else 0))
                    sp.dma_start(out[0][t * P:(t + 1) * P, half], h2[:, t, half]).then_inc(out_done, 16)
            sp.wait_ge(out_done, 16 * (NT + 1))

        @block.gpsimd
        def _(pool):
            nc.gpsimd.memset(epss[:, 0:1], RMS_EPS).then_inc(eps_set, 1)
            nc.gpsimd.memset(epss[:, 1:2], LN_EPS).then_inc(eps_set, 1)
            for t in range(NT):
                if t == 0:
                    pool.wait_ge(krot_set, 2)
                    pool.wait_ge(xt_low, KD)
                    pool.wait_ge(xt_high, KD)
                nc.gpsimd.tensor_copy(kf[:, t, :, NOPE:QK],
                                      krot[:, t, :].unsqueeze(1).broadcast_to([P, HEADS, ROPE])).then_inc(krot_spread, 1)
            pool.wait_ge(const_in, 64)
            for h in range(HEADS):
                if h >= 2:
                    pool.wait_ge(max_set, 3 * (HEADS + h - 1))
                nc.gpsimd.tensor_scalar(bias[:, h % 2, :], dist, SLOPES[h], None, ALU.mult).then_inc(pchain, 1)
                pool.wait_ge(pchain, h + 1)
                nc.gpsimd.tensor_tensor(bias[:, h % 2, :], bias[:, h % 2, :], lcount, ALU.add).then_inc(bias_set, 1)
            pool.wait_ge(bias_set, HEADS)
            pool.wait_ge(max_set, 6 * HEADS)
            pool.dma_start(lng, a["ln1_g"].broadcast_to([P, D])).then_inc(ln_in, 16)
            pool.dma_start(lnb, a["ln1_b"].broadcast_to([P, D])).then_inc(ln_in, 16)
            pool.wait_ge(mix_low, KD)
            for t in range(NT):
                pool.dma_start(xtok[:, t, :], a["x"][0][t * P:(t + 1) * P, :]).then_inc(x2_in[t], 16)
            for t in range(NT):
                pool.wait_ge(h_set, t + 1)
                pool.dma_start(spill[:, t, :], hres[:, t, :]).then_inc(spilled, 16)
            pool.wait_ge(f_low, KF)
            pool.wait_ge(spilled, 16 * NT)
            pool.dma_start(h2, spill).then_inc(h2_in, 16)
            pool.dma_start(lng, a["ln2_g"].broadcast_to([P, D])).then_inc(ln2_in, 16)
            pool.dma_start(lnb, a["ln2_b"].broadcast_to([P, D])).then_inc(ln2_in, 16)

        @block.scalar
        def _(act):
            copy = ACT.Copy

            def prep(u):
                src, high, _ = split_dest(u)
                act.wait_ge(raw_in[POS[u] % NRAW], RAW_COUNT[u])
                if u in RING and RING[u] >= NRING:
                    act.wait_ge(unit_done, RING[u] - NRING + 1)
                if u[0] == "out":
                    if u[1] == 0:
                        act.wait_ge(unit_done, RING[("proj", NPROJ - 1)] + 1)
                        act.wait_ge(pv_ps, 2 * HEADS)
                    nc.scalar.activation(wout[0][:, u[1], 0, :], src[:, 0:S], copy)
                    nc.scalar.activation(wout[1][:, u[1], 0, :], src[:, S:D], copy).then_inc(w_high, 1)
                    return
                if u[0] == "ff2" and u[1] >= KF - LAST:
                    j = u[1] - (KF - LAST)
                    act.wait_ge(unit_done, RING[("ff2", 2 * j + 1)] + 1)
                nc.scalar.activation(high, src, copy).then_inc(w_high, 1)

            for k in range(KD):
                act.wait_ge(xt_ps, k + 1)
                nc.scalar.activation(xt[:, k, 0, :], bank[2 + k % 6][:, :], copy).then_inc(xt_high, 1)
                if k in (0, 4, 7):
                    prep(UNITS[(0, 4, 7).index(k)])

            def norm(c):
                act.wait_ge(sum_ps, c + 1)
                act.wait_ge(eps_set, 2)
                nc.scalar.activation(rinv[:, c, :], bank[6 + c][:, :], ACT.Sqrt, bias=epss[:, 0:1],
                                     scale=1.0 / (QL, KVL)[c]).then_inc(dev_set, 1)
                for m in (range(NQL), range(NQL, NLORA))[c]:
                    act.wait_ge(norm_set, m + 1)
                    nc.scalar.activation(lora[:, m, 0, :], ltmp[:, m % 2, :], copy).then_inc(norm_high, 1)

            act.wait_ge(xt_low, KD)
            for m in range(NLORA + 1):
                act.wait_ge(unit_done, m + 1)
                ps = bank[m % 2]
                if m < NLORA:
                    nc.scalar.activation(lraw[:, m, :], ps[:, :], copy).then_inc(acc_read, 1)
                    act.wait_ge(acc_read, m + 1)
                    if m >= 4:
                        act.wait_ge(sum_ps, 1)
                    nc.scalar.activation(sqh[:, m % 4, 0, :], lraw[:, m, :], ACT.Square).then_inc(sq_high, 1)
                else:
                    nc.scalar.activation(krt, ps[0:ROPE, :], copy).then_inc(acc_read, 1)
                prep(IN_RING[m + 3])
                if m < NQL:
                    prep(("uq", m))
                if m == NQL:
                    norm(0)

            def unit_event(p):
                act.wait_ge(unit_done, RING[("proj", p)] + 1)
                ps = bank[(NLORA + 1 + p) % 2][:, :]
                if p < 12:
                    nc.scalar.activation(dilf[:, p % 3, p // 3, :], ps, copy).then_inc(acc_read, 1)
                else:
                    nc.scalar.activation(z[:, p - 12, :], ps, ACT.Identity, bias=bg[:, p - 12:p - 11]).then_inc(acc_read, 1)
                prep(IN_RING[RING[("proj", p)] + 3])

            norm(1)
            act.wait_ge(sum_ps, 2)
            act.wait_ge(sq_low, NLORA)
            prep(("ukv", 0))
            prep(("ukv", 1))
            for i in range(4 * NT):
                t, c, b = (i % 8) // 2, i % 2, 2 + i % 6
                act.wait_ge(qkv_ps, i + 1)
                if i < 8:
                    nc.scalar.activation(qf[:, t, 4 * c:4 * c + 4, :],
                                         bank[b][:, 0:384].rearrange("p (h d) -> p h d", h=4), copy).then_inc(qkv_read, 1)
                else:
                    ps = bank[b][:, :].rearrange("p (h d) -> p h d", h=4)
                    nc.scalar.activation(kf[:, t, 4 * c:4 * c + 4, 0:NOPE], ps[:, :, 0:NOPE], copy)
                    nc.scalar.activation(vf[:, t, 4 * c:4 * c + 4, :], ps[:, :, NOPE:NOPE + VD], copy).then_inc(qkv_read, 1)

            def transposed(kind, g):
                i = TI[(kind, g)]
                ps = TB[TBANK[kind]]
                act.wait_ge(t_ps, i + 1)
                if kind in ("q", "k"):
                    dst, src = qkb[0:QK, g % 2, "qk".index(kind), 0, :], ps[0:QK, :]
                elif kind == "v":
                    dst = vb[:, 0, :, :].rearrange("p t (c d) -> p t c d", c=3)[:, :, 0:3:2, :]
                    src = ps[:, :].rearrange("p (t c d) -> p t c d", t=NT, c=2)
                else:
                    o, w = {"p0": (0, 512), "p1": (512, 384), "p2": (896, 384)}[kind]
                    dst, src = ptb[:, 0, o:o + w], ps[:, 0:w]
                nc.scalar.activation(dst, src, copy).then_inc(t_high, 1)

            transposed("q", 0)
            transposed("k", 0)
            unit_event(0)
            for g in range(2 * HEADS):
                if g % 2 == 0 and g:
                    act.wait_ge(pv_ps, g)
                    nc.scalar.activation(ot[:, g // 2 - 1, 0, :], OB[:, :], copy).then_inc(o_high, 1)
                if g % 2 == 0 and g < HEADS:
                    act.wait_ge(qkv_read, 4 * NT)
                    act.wait_ge(vzero, 1)
                    nc.scalar.activation(vb[:, 0, :, :].rearrange("p t (c d) -> p t c d", c=3)[:, :, 0:3:2, :],
                                         vf[:, :, g:g + 2, :], copy).then_inc(v_high, 1)
                if g + 1 < HEADS:
                    transposed("q", g + 1)
                    transposed("k", g + 1)
                if g >= HEADS and g % 2 == 0:
                    transposed("v", g)
                for n, (b, blocks) in enumerate(SORDER):
                    act.wait_ge(max_set, 3 * g + n + 1)
                    for qb in blocks:
                        o, w = SPLACE[qb][1], P * (qb + 1)
                        p = pbuf[:, POFF[qb]:POFF[qb] + w]
                        src, scale = (SB[b][:, o:o + w], MLA_SCALE) if g < HEADS else (p, 1.0)
                        nc.scalar.activation(p, src, ACT.Exp, bias=nm[:, qb:qb + 1], scale=scale,
                                             accum_out=rs[:, qb:qb + 1]).then_inc(exp_set, 1)
                unit_event(PRE + (3 * g) // 2)
                transposed("p0", g)
                transposed("p1", g)
                transposed("p2", g)
                if g >= HEADS - 1 and g % 2 == 1 and g < 2 * HEADS - 1:
                    j = (g - HEADS + 1) // 2
                    act.wait_ge(acc_read, NLORA + 1 + 3 * j + 3)
                    nc.scalar.activation(qkb[:, j % 2, :, 0, :], dilf[:, 0:2, j, :], copy).then_inc(qk_high, 1)
                if g % 2 == 1:
                    unit_event(PRE + 1 + (3 * g) // 2)
            act.wait_ge(pv_ps, 2 * HEADS)
            nc.scalar.activation(ot[:, HEADS - 1, 0, :], OB[:, :], copy).then_inc(o_high, 1)
            for p in range(PRE + 3 * HEADS, NPROJ):
                unit_event(p)

            act.wait_ge(acc_read, NLORA + 1 + NPROJ)
            for m in range(KD):
                for b in range(2):
                    nc.scalar.activation(z[:, b * KD + m, :], z[:, b * KD + m, :], ACT.Sigmoid).then_inc(gate_set, 1)
                act.wait_ge(unit_done, RING[("y", m)] + 1)
                if m + 3 < KD:
                    prep(("y", m + 3))
                prep(("out", m))
                act.wait_ge(mix_set, m + 1)
                nc.scalar.activation(mixed[:, m, 0, :], z[:, m, :], copy).then_inc(mix_high, 1)
            for m in range(3):
                prep(("ff1", m))

            def deviation(t):
                act.wait_ge(var_set, t + 1)
                nc.scalar.activation(std[:, t:t + 1], mv[:, t, 1:2], ACT.Sqrt, bias=epss[:, 1:2]).then_inc(dev1_set, 1)

            deviation(0)
            deviation(1)
            for t in range(NT):
                if t == 1:
                    deviation(2)
                for c in range(2):
                    act.wait_ge(ht_ps, 2 * t + c + 1)
                    nc.scalar.activation(xt[:, 4 * c:4 * c + 4, 0, t * P:(t + 1) * P],
                                         bank[4 + 2 * (t % 2) + c][:, :].rearrange("p (k n) -> p k n", k=4),
                                         copy).then_inc(ht_high, 1)
                if t == 2:
                    deviation(3)

            for m in range(KF):
                act.wait_ge(unit_done, RING[("ff1", m)] + 1)
                if m >= 2:
                    act.wait_ge(f_low, m - 1)
                if m == 16:
                    act.wait_ge(spilled, 16 * NT)
                if m == 0:
                    act.wait_ge(h_set, NT)
                nc.scalar.activation(relu[:, m % 2, :], bank[m % 4][:, :], ACT.Relu).then_inc(relu_set, 1)
                act.wait_ge(relu_set, m + 1)
                nc.scalar.activation(ff[:, m, 0, :], relu[:, m % 2, :], ACT.Square).then_inc(f_high, 1)
                prep(("ff1", m + 3) if m + 3 < KF else ("ff2", m + 3 - KF))
            for k in range(KF - LAST):
                if k + 3 < KF - LAST:
                    prep(("ff2", k + 3))
                if k % 3 == 2:
                    prep(("ff2", KF - LAST + k // 3))
            for t in range(NT):
                act.wait_ge(var2_set, t + 1)
                nc.scalar.activation(std[:, t:t + 1], mv[:, t, 1:2], ACT.Sqrt, bias=epss[:, 1:2]).then_inc(dev2_set, 1)

        @block.vector
        def _(dve):
            links = [0]

            def link(ins):
                links[0] += 1
                ins.then_inc(dchain, 1)
                dve.wait_ge(dchain, links[0])

            def low(dst, src, high, done):
                nc.vector.tensor_tensor(dst, src, high.bitcast(F32), ALU.subtract).then_inc(done, 1)

            def prep(u):
                src, high, lo = split_dest(u)
                dve.wait_ge(w_high, POS[u] + 1)
                if u[0] == "out":
                    for n in range(2):
                        ins = nc.vector.tensor_tensor(wout[n][:, u[1], 1, :], src[:, n * S:(n + 1) * S],
                                                      wout[n][:, u[1], 0, :].bitcast(F32), ALU.subtract)
                    ins.then_inc(w_low, 1)
                    return
                low(lo, src, high, w_low)

            nc.vector.memset(ones[:, :].bitcast(F32), 1.0).then_inc(ones_set, 1)
            nc.vector.memset(vb.bitcast(F32), 0.0).then_inc(vzero, 1)
            for k in range(KD):
                dve.wait_ge(xt_high, k + 1)
                low(xt[:, k, 1, :], bank[2 + k % 6][:, :], xt[:, k, 0, :], xt_low)
                if k in (0, 4, 7):
                    prep(UNITS[(0, 4, 7).index(k)])

            def norm(c):
                dve.wait_ge(dev_set, c + 1)
                dve.wait_ge(const_in, 64)
                link(nc.vector.reciprocal(rinv[:, c, :], rinv[:, c, :]))
                for m in (range(NQL), range(NQL, NLORA))[c]:
                    if m >= 2:
                        dve.wait_ge(norm_low, m - 1)
                    nc.vector.scalar_tensor_tensor(out=ltmp[:, m % 2, :], in0=lraw[:, m, :], scalar=gq[:, m:m + 1],
                                                   in1=rinv[:, c, :], op0=ALU.mult, op1=ALU.mult).then_inc(norm_set, 1)
                    dve.wait_ge(norm_high, m + 1)
                    low(lora[:, m, 1, :], ltmp[:, m % 2, :], lora[:, m, 0, :], norm_low)

            for m in range(NLORA + 1):
                if m < NLORA:
                    dve.wait_ge(acc_read, m + 1)
                    if m >= 2:
                        dve.wait_ge(sq_low, m - 1)
                    link(nc.vector.tensor_tensor(sqt[:, m % 2, :], lraw[:, m, :], lraw[:, m, :], ALU.mult))
                    dve.wait_ge(sq_high, m + 1)
                    low(sqh[:, m % 4, 1, :], sqt[:, m % 2, :], sqh[:, m % 4, 0, :], sq_low)
                prep(IN_RING[m + 3])
                if m < NQL:
                    prep(("uq", m))
                if m == NQL:
                    norm(0)

            def rotate(lo_out, hi_out, t1, t2, c, s):
                shape = [P] + list(t1.shape[1:])
                prod = [rtmp[:, n, :, :] if len(shape) == 3 and shape[1] == HEADS else
                        pbuf[:, 1536 + n * NT * HALF:1536 + (n + 1) * NT * HALF].rearrange("p (t i) -> p t i", t=NT)
                        for n in range(4)]
                nc.vector.tensor_tensor(prod[0], t1, c, ALU.mult)
                nc.vector.tensor_tensor(prod[1], t2, s, ALU.mult)
                nc.vector.tensor_tensor(prod[2], t1, s, ALU.mult)
                link(nc.vector.tensor_tensor(prod[3], t2, c, ALU.mult))
                nc.vector.tensor_tensor(lo_out, prod[0], prod[1], ALU.subtract)
                return nc.vector.tensor_tensor(hi_out, prod[2], prod[3], ALU.add)

            def unit_event(p):
                prep(IN_RING[RING[("proj", p)] + 3])

            dve.wait_ge(krt_ps, 1)
            dve.wait_ge(small_in, 16)
            kps = bank[5][:, 0:NT * ROPE].rearrange("p (t d) -> p t d", t=NT)
            rotate(krot[:, :, 0:HALF], krot[:, :, HALF:ROPE], kps[:, :, 0:HALF], kps[:, :, HALF:ROPE],
                   cos, sin).then_inc(krot_set, 2)
            norm(1)
            prep(("ukv", 0))
            prep(("ukv", 1))
            for t in range(NT):
                dve.wait_ge(qkv_read, 2 * t + 2)
                if t:
                    dve.wait_ge(q_rot, t)
                q1, q2 = qf[:, t, :, NOPE:NOPE + HALF], qf[:, t, :, NOPE + HALF:QK]
                rotate(q1, q2, q1, q2, cos[:, t, :].unsqueeze(1).broadcast_to([P, HEADS, HALF]),
                       sin[:, t, :].unsqueeze(1).broadcast_to([P, HEADS, HALF])).then_inc(q_rot, 1)

            def transposed(kind, g):
                i = TI[(kind, g)]
                ps = TB[TBANK[kind]]
                dve.wait_ge(t_high, i + 1)
                if kind in ("q", "k"):
                    b = qkb[0:QK, g % 2, "qk".index(kind), :, :]
                    low(b[:, 1, :], ps[0:QK, :], b[:, 0, :], t_low)
                elif kind == "v":
                    v = vb[:, :, :, :].rearrange("p s t (c d) -> p s t c d", c=3)[:, :, :, 0:3:2, :]
                    low(v[:, 1], ps[:, :].rearrange("p (t c d) -> p t c d", t=NT, c=2), v[:, 0], t_low)
                else:
                    o, w = {"p0": (0, 512), "p1": (512, 384), "p2": (896, 384)}[kind]
                    low(ptb[:, 1, o:o + w], ps[:, 0:w], ptb[:, 0, o:o + w], t_low)

            transposed("q", 0)
            transposed("k", 0)
            unit_event(0)
            for g in range(2 * HEADS):
                if g:
                    dve.wait_ge(max_set, 3 * g)
                    dve.wait_ge(exp_set, 4 * g)
                for n, (b, blocks) in enumerate(SORDER):
                    dve.wait_ge(sc_ps, 3 * g + n + 1)
                    for qb in blocks:
                        o, w = SPLACE[qb][1], P * (qb + 1)
                        ps = SB[b][:, o:o + w]
                        if g < HEADS:
                            diag = SB[b][:, o + w - P:o + w]
                            link(nc.vector.tensor_tensor(diag, diag, causal, ALU.add))
                            ins = nc.vector.reduce_max(mx[:, qb:qb + 1], ps, AX.X)
                        else:
                            h = g - HEADS
                            dve.wait_ge(bias_set, h + 1)
                            p = pbuf[:, POFF[qb]:POFF[qb] + w]
                            link(nc.vector.scalar_tensor_tensor(out=p, in0=ps, scalar=DIL_SCALE, in1=bias[:, h % 2, S - w:S],
                                                                op0=ALU.mult, op1=ALU.add))
                            ins = nc.vector.reduce_max(mx[:, qb:qb + 1], p, AX.X)
                    link(ins)
                    nc.vector.tensor_scalar(nm[:, blocks[-1]:blocks[0] + 1], mx[:, blocks[-1]:blocks[0] + 1],
                                            -MLA_SCALE if g < HEADS else -1.0, None, ALU.mult).then_inc(max_set, 1)
                if g % 2 == 0 and g:
                    dve.wait_ge(o_high, g // 2)
                    low(ot[:, g // 2 - 1, 1, :], OB[:, :], ot[:, g // 2 - 1, 0, :], o_low)
                for n, (b, blocks) in enumerate(SORDER):
                    dve.wait_ge(exp_set, 4 * g + (1, 2, 4)[n])
                    if g:
                        dve.wait_ge(p_set, 3 * g)
                    link(nc.vector.reciprocal(rr[:, blocks[-1]:blocks[0] + 1], rs[:, blocks[-1]:blocks[0] + 1]))
                    for qb in blocks:
                        p = pbuf[:, POFF[qb]:POFF[qb] + P * (qb + 1)]
                        ins = nc.vector.tensor_scalar(p, p, rr[:, qb:qb + 1], None, ALU.mult)
                    ins.then_inc(p_set, 1)
                if g + 1 < HEADS:
                    transposed("q", g + 1)
                    transposed("k", g + 1)
                if g % 2 == 0 and g < HEADS:
                    dve.wait_ge(v_high, g // 2 + 1)
                    v = vb[:, :, :, :].rearrange("p s t (c d) -> p s t c d", c=3)[:, :, :, 0:3:2, :]
                    low(v[:, 1], vf[:, :, g:g + 2, :], v[:, 0], v_low)
                if g >= HEADS and g % 2 == 0:
                    transposed("v", g)
                transposed("p0", g)
                transposed("p1", g)
                transposed("p2", g)
                if g >= HEADS - 1 and g % 2 == 1 and g < 2 * HEADS - 1:
                    j = (g - HEADS + 1) // 2
                    dve.wait_ge(qk_high, j + 1)
                    low(qkb[:, j % 2, :, 1, :], dilf[:, 0:2, j, :], qkb[:, j % 2, :, 0, :], qk_low)
                unit_event(PRE + (3 * g) // 2)
                if g % 2 == 1:
                    unit_event(PRE + 1 + (3 * g) // 2)
            dve.wait_ge(o_high, HEADS)
            low(ot[:, HEADS - 1, 1, :], OB[:, :], ot[:, HEADS - 1, 0, :], o_low)
            for p in range(PRE + 3 * HEADS, NPROJ):
                unit_event(p)

            for m in range(KD):
                dve.wait_ge(unit_done, RING[("y", m)] + 1)
                dve.wait_ge(gate_set, 2 * m + 2)
                ya, yb = bank[2 * (m % 2)], bank[2 * (m % 2) + 1]
                nc.vector.tensor_tensor(z[:, m, :], ya[:, :], z[:, m, :], ALU.mult).then_inc(mix_read, 1)
                nc.vector.tensor_tensor(z[:, KD + m, :], yb[:, :], z[:, KD + m, :], ALU.mult).then_inc(mix_read, 1)
                dve.wait_ge(mix_read, 2 * m + 2)
                nc.vector.tensor_tensor(z[:, m, :], z[:, m, :], z[:, KD + m, :], ALU.add).then_inc(mix_set, 1)
                if m + 3 < KD:
                    prep(("y", m + 3))
                prep(("out", m))
                dve.wait_ge(mix_high, m + 1)
                low(mixed[:, m, 1, :], z[:, m, :], mixed[:, m, 0, :], mix_low)
            for m in range(3):
                prep(("ff1", m))

            def normalise(buf, t, dev, part=slice(0, D)):
                link(nc.vector.scalar_tensor_tensor(out=buf[:, t, part], in0=buf[:, t, part], scalar=mv[:, t, 0:1],
                                                    in1=lng[:, part], op0=ALU.subtract, op1=ALU.mult))
                if part.start == 0:
                    dve.wait_ge(dev, t + 1)
                    link(nc.vector.reciprocal(rstd[:, t:t + 1], std[:, t:t + 1]))
                return nc.vector.scalar_tensor_tensor(out=buf[:, t, part], in0=buf[:, t, part], scalar=rstd[:, t:t + 1],
                                                      in1=lnb[:, part], op0=ALU.mult, op1=ALU.add)

            def low_h(t):
                for c in range(2):
                    dve.wait_ge(ht_high, 2 * t + c + 1)
                    dst = xt[:, 4 * c:4 * c + 4, :, t * P:(t + 1) * P]
                    low(dst[:, :, 1, :], bank[4 + 2 * (t % 2) + c][:, :].rearrange("p (k n) -> p k n", k=4), dst[:, :, 0, :], ht_low)

            for n in range(2):
                for t in range(NT):
                    half = slice(n * S, (n + 1) * S)
                    dve.wait_ge(out_ps, n * NT + t + 1)
                    if n == 0:
                        dve.wait_ge(x2_in[t], 16)
                    nc.vector.scalar_tensor_tensor(out=hres[:, t, half], in0=xtok[:, t, half], scalar=ALPHA,
                                                   in1=bank[(n * NT + t) % 4][:, :], op0=ALU.mult, op1=ALU.add).then_inc(res_set, 1)
                    dve.wait_ge(res_set, n * NT + t + 1)
                    link(nc.vector.bn_stats(bns[:, t, n, :], hres[:, t, half]))
                    if n == 1:
                        nc.vector.bn_aggr(mv[:, t, :], bns[:, t, :, :].rearrange("p a b -> p (a b)")).then_inc(var_set, 1)
                        if t == 0:
                            dve.wait_ge(ln_in, 32)
                        dve.wait_ge(var_set, t + 1)
                        if t == NT - 1:
                            low_h(NT - 2)
                        normalise(hres, t, dev1_set).then_inc(h_set, 1)
                        if 0 < t < NT - 1:
                            low_h(t - 1)
            low_h(NT - 1)

            for m in range(KF):
                dve.wait_ge(relu_set, m + 1)
                if m >= 2:
                    dve.wait_ge(f_low, m - 1)
                link(nc.vector.tensor_tensor(fsq[:, m % 2, :], relu[:, m % 2, :], relu[:, m % 2, :], ALU.mult))
                dve.wait_ge(f_high, m + 1)
                low(ff[:, m, 1, :], fsq[:, m % 2, :], ff[:, m, 0, :], f_low)
                prep(("ff1", m + 3) if m + 3 < KF else ("ff2", m + 3 - KF))
            for k in range(KF - LAST):
                if k + 3 < KF - LAST:
                    prep(("ff2", k + 3))
                if k % 3 == 2:
                    prep(("ff2", KF - LAST + k // 3))

            for t in range(NT):
                for n in range(2):
                    half = slice(n * S, (n + 1) * S)
                    dve.wait_ge(ff2_ps, 2 * t + n + 1)
                    dve.wait_ge(h2_in, 16)
                    link(nc.vector.scalar_tensor_tensor(out=h2[:, t, half], in0=h2[:, t, half], scalar=ALPHA,
                                                        in1=bank[2 * t + n][:, :], op0=ALU.mult, op1=ALU.add))
                    link(nc.vector.bn_stats(bns[:, t, n, :], h2[:, t, half]))
                nc.vector.bn_aggr(mv[:, t, :], bns[:, t, :, :].rearrange("p a b -> p (a b)")).then_inc(var2_set, 1)
                dve.wait_ge(ln2_in, 32)
                dve.wait_ge(var2_set, t + 1)
                if t < NT - 1:
                    normalise(h2, t, dev2_set).then_inc(y_set, 1)
                else:
                    for n in range(2):
                        normalise(h2, t, dev2_set, slice(n * S, (n + 1) * S)).then_inc(y_set, 1)

        @block.tensor
        def _(pe):
            PASSES = ((0, 0), (0, 1), (1, 0))

            def product(out_, stationary, moving, first, last):
                for n, (a_, b_) in enumerate(PASSES):
                    ins = nc.tensor.matmul(out_, stationary(a_), moving(b_), start=first and n == 0, stop=last and n == 2)
                return ins

            def ring(u, lo, hi):
                slot = RING[u] % NRING
                return lambda s: (ring_h, ring_l)[s][:, slot, lo:hi]

            pe.wait_ge(small_in, 16)
            for k in range(KD):
                if k >= 6:
                    pe.wait_ge(xt_low, k - 5)
                for t in range(NT):
                    if k == 0:
                        pe.wait_ge(x_in[t], 16)
                    ins = nc.tensor.transpose(bank[2 + k % 6][:, t * P:(t + 1) * P], xtok[:, t, k * P:(k + 1) * P], ident)
                ins.then_inc(xt_ps, 1)

            def k_step(u, k, acc):
                if k == 0:
                    pe.wait_ge(w_low, POS[u] + 1)
                    if acc >= 2:
                        pe.wait_ge(acc_read, acc - 1)
                ins = product(bank[acc % 2][:, :], ring(u, k * P, (k + 1) * P), lambda s: xt[:, k, s, :], k == 0, k == KD - 1)
                if k == KD - 1:
                    ins.then_inc(unit_done, 1)

            def square_sum(c):
                tiles = (range(NQL), range(NQL, NLORA))[c]
                pe.wait_ge(sq_low, tiles[-1] + 1)
                for m in tiles:
                    for s in range(2):
                        ins = nc.tensor.matmul(bank[6 + c][:, :], ones[:, :], sqh[:, m % 4, s, :],
                                               start=(m == tiles[0] and s == 0), stop=(m == tiles[-1] and s == 1))
                ins.then_inc(sum_ps, 1)

            pe.wait_ge(ones_set, 1)
            for m in range(NLORA + 1):
                for k in range(KD):
                    if m == 0:
                        pe.wait_ge(xt_low, k + 1)
                    k_step(("lora", m), k, m)
                if m == 3:
                    square_sum(0)
            filled = [0]

            def fill(steps):
                for _ in range(steps):
                    p, k = divmod(filled[0], KD)
                    k_step(("proj", p), k, NLORA + 1 + p)
                    filled[0] += 1

            square_sum(1)
            pe.wait_ge(acc_read, NLORA + 1)
            for t in range(NT):
                ins = nc.tensor.transpose(bank[5][:, t * ROPE:(t + 1) * ROPE], krt[:, t * P:(t + 1) * P], ident[0:ROPE, 0:ROPE])
            ins.then_inc(krt_ps, 1)


            for i in range(4 * NT):
                t, c, b = (i % 8) // 2, i % 2, 2 + i % 6
                if i >= 6:
                    pe.wait_ge(qkv_read, i - 5)
                elif b == 5:
                    pe.wait_ge(krot_set, 2)
                elif b >= 6:
                    pe.wait_ge(dev_set, b - 5)
                if i == 0:
                    pe.wait_ge(norm_low, NQL)
                    pe.wait_ge(w_low, POS[("uq", NQL - 1)] + 1)
                if i == 8:
                    pe.wait_ge(norm_low, NLORA)
                    pe.wait_ge(w_low, POS[("ukv", NKVL - 1)] + 1)
                if i < 8:
                    for k in range(NQL):
                        ins = product(bank[b][:, 0:384], lambda s: lora[:, k, s, t * P:(t + 1) * P],
                                      lambda s: uq[k][:, s, c * 384:(c + 1) * 384], k == 0, k == NQL - 1)
                    ins.then_inc(qkv_ps, 1)
                else:
                    for k in range(NKVL):
                        ins = product(bank[b][:, :], lambda s: lora[:, NQL + k, s, t * P:(t + 1) * P],
                                      lambda s: ukv[:, k, s, c * 512:(c + 1) * 512], k == 0, k == NKVL - 1)
                    ins.then_inc(qkv_ps, 1)

            def t_bank(kind, g):
                if TPREV[(kind, g)] is not None:
                    pe.wait_ge(t_low, TPREV[(kind, g)] + 1)
                return TB[TBANK[kind]]

            def transpose_qk(h):
                for kind, src in (("q", qf), ("k", kf)):
                    ps = t_bank(kind, h)
                    for t in range(NT):
                        ins = nc.tensor.transpose(ps[0:QK, t * P:(t + 1) * P], src[:, t, h, :], ident)
                    ins.then_inc(t_ps, 1)

            def transpose_v(g):
                j = (g - HEADS) // 2
                ps = t_bank("v", g)
                pe.wait_ge(acc_read, NLORA + 1 + 3 * j + 3)
                for t in range(NT):
                    ins = nc.tensor.transpose(ps[:, t * P:(t + 1) * P], dilf[:, 2, j, t * P:(t + 1) * P], ident)
                ins.then_inc(t_ps, 1)

            def scores(g):
                if g < HEADS:
                    buf, rows = g % 2, slice(0, QK)
                    pe.wait_ge(t_low, TI[("k", g)] + 1)
                else:
                    j = (g - HEADS) // 2
                    buf, rows = j % 2, slice(64 * (g % 2), 64 * (g % 2) + 64)
                    pe.wait_ge(qk_low, j + 1)
                if g:
                    pe.wait_ge(exp_set, 4 * g)
                for b, blocks in SORDER:
                    for qb in blocks:
                        o, w = SPLACE[qb][1], P * (qb + 1)
                        ins = product(SB[b][:, o:o + w], lambda s: qkb[rows, buf, 0, s, qb * P:(qb + 1) * P],
                                      lambda s: qkb[rows, buf, 1, s, 0:w], True, True)
                    ins.then_inc(sc_ps, 1)

            def transpose_p(g, kind, key_blocks):
                ps = t_bank(kind, g)
                base = KOFF[key_blocks[0]]
                for kb in key_blocks:
                    for qb in range(kb, NT):
                        o = KOFF[kb] - base + (qb - kb) * P
                        ins = nc.tensor.transpose(ps[:, o:o + P], pbuf[:, POFF[qb] + kb * P:POFF[qb] + (kb + 1) * P], ident)
                ins.then_inc(t_ps, 1)

            def weighted_values(g):
                if g % 2 == 0 and g:
                    pe.wait_ge(o_low, g // 2)
                if g < HEADS:
                    pe.wait_ge(v_low, g // 2 + 1)
                for kb in range(NT):
                    pe.wait_ge(t_low, TI[({0: "p0", 1: "p1"}.get(kb, "p2"), g)] + 1)
                    w = S - kb * P
                    for n, (a_, b_) in enumerate(PASSES):
                        ins = nc.tensor.matmul(OB[:, kb * P:S], vb[:, a_, kb, 64 * (g % 2):64 * (g % 2) + P],
                                               ptb[:, b_, KOFF[kb]:KOFF[kb] + w],
                                               start=(g % 2 == 0 and kb == 0 and n == 0),
                                               stop=(g % 2 == 1 and kb == NT - 1 and n == 2))
                ins.then_inc(pv_ps, 1)

            fill(3)
            pe.wait_ge(q_rot, NT)
            pe.wait_ge(qkv_read, 4 * NT)
            pe.wait_ge(krot_spread, NT)
            transpose_qk(0)
            fill(KD * PRE - 3)
            for g in range(2 * HEADS):
                scores(g)
                if g + 1 < HEADS:
                    transpose_qk(g + 1)
                if g >= HEADS and g % 2 == 0:
                    transpose_v(g)
                fill(9)
                pe.wait_ge(p_set, 3 * g + 3)
                transpose_p(g, "p0", (0,))
                transpose_p(g, "p1", (1,))
                fill(2)
                transpose_p(g, "p2", (2, 3))
                fill(1)
                weighted_values(g)
            fill(KD * NPROJ - filled[0])

            for m in range(KD):
                u = ("y", m)
                pe.wait_ge(w_low, POS[u] + 1)
                if m == 0:
                    pe.wait_ge(o_low, HEADS)
                    pe.wait_ge(acc_read, NLORA + 1 + NPROJ)
                if m >= 2:
                    pe.wait_ge(mix_read, 2 * (m - 1))
                for k in range(HEADS):
                    ins = product(bank[2 * (m % 2) + k // 4][:, :], ring(u, k * P, (k + 1) * P),
                                  lambda s: ot[:, k, s, :], k % 4 == 0, k % 4 == 3)
                ins.then_inc(unit_done, 1)

            def transpose_h(t):
                pe.wait_ge(h_set, t + 1)
                for c in range(2):
                    if t >= 2:
                        pe.wait_ge(ht_low, 2 * (t - 2) + c + 1)
                    for k in range(4):
                        ins = nc.tensor.transpose(bank[4 + 2 * (t % 2) + c][:, k * P:(k + 1) * P],
                                                  hres[:, t, (4 * c + k) * P:(4 * c + k + 1) * P], ident)
                    ins.then_inc(ht_ps, 1)

            for n in range(2):
                for t in range(NT):
                    i = n * NT + t
                    if i >= 4:
                        pe.wait_ge(res_set, i - 3)
                    else:
                        pe.wait_ge(mix_read, 2 * KD if i >= 2 else 2 * KD - 2)
                    for k in range(KD):
                        if i == 0:
                            pe.wait_ge(w_low, POS[("out", k)] + 1)
                            pe.wait_ge(mix_low, k + 1)
                        ins = product(bank[i % 4][:, :], lambda s: mixed[:, k, s, t * P:(t + 1) * P],
                                      lambda s: wout[n][:, k, s, :], k == 0, k == KD - 1)
                    ins.then_inc(out_ps, 1)
                    if n == 1 and t >= 2:
                        transpose_h(t - 2)
            transpose_h(NT - 2)

            def hidden(m, tokens):
                u = ("ff1", m)
                pe.wait_ge(w_low, POS[u] + 1)
                if m < 4:
                    pe.wait_ge(res_set, 2 * NT)
                else:
                    pe.wait_ge(relu_set, m - 3)
                for k in range(KD):
                    ins = product(bank[m % 4][:, tokens], ring(u, k * P, (k + 1) * P), lambda s: xt[:, k, s, tokens],
                                  k == 0, k == KD - 1)
                return ins

            early = slice(0, (NT - 1) * P)
            pe.wait_ge(ht_low, 2 * (NT - 1))
            hidden(0, early)
            transpose_h(NT - 1)
            hidden(1, early)
            pe.wait_ge(ht_low, 2 * NT)
            for m in range(KF):
                hidden(m, slice((NT - 1) * P, S) if m < 2 else slice(0, S)).then_inc(unit_done, 1)

            for k in range(KF - LAST):
                u = ("ff2", k)
                pe.wait_ge(w_low, POS[u] + 1)
                pe.wait_ge(f_low, k + 1)
                for t in (2, 3, 0, 1):
                    if k == 0 and t == 0:
                        pe.wait_ge(relu_set, KF)
                    for a_, b_ in PASSES:
                        for n in range(2):
                            ins = nc.tensor.matmul(bank[2 * t + n][:, :], ff[:, k, a_, t * P:(t + 1) * P],
                                                   ring(u, n * S, (n + 1) * S)(b_), start=(k == 0 and a_ == 0 and b_ == 0), stop=False)
                ins.then_inc(unit_done, 1)
            for t in range(NT):
                for n in range(2):
                    for j in range(LAST):
                        k = KF - LAST + j
                        if t == 0 and n == 0:
                            pe.wait_ge(w_low, POS[("ff2", k)] + 1)
                            pe.wait_ge(f_low, k + 1)
                        w2 = lambda s: ff[:, 2 * j + s, n, :]
                        ins = product(bank[2 * t + n][:, :], lambda s: ff[:, k, s, t * P:(t + 1) * P], w2, False, j == LAST - 1)
                    ins.then_inc(ff2_ps, 1)


INPUTS = ["x", "w_in", "b_gate", "g_q_a", "w_uq", "g_kv_a", "w_ukv", "w_o_mla", "w_o_dil", "w_out",
          "ln1_g", "ln1_b", "w_ff1", "w_ff2", "ln2_g", "ln2_b"]


def kernel(**inputs):
    import concourse.bacc as bacc
    from concourse.bass_utils import run_bass_kernel_spmd as run

    nc = bacc.Bacc("TRN2", target_bir_lowering=False, num_devices=1)
    arrays, aps = {}, {}
    for name in INPUTS:
        arrays[f"in_{name}"] = np.ascontiguousarray(inputs[name])
    arrays["in_const"] = constants()
    for name, v in arrays.items():
        aps[name[3:]] = nc.dram_tensor(name, v.shape, F32, kind="ExternalInput").ap()
    y = nc.dram_tensor("out_y", (1, S, D), F32, kind="ExternalOutput").ap()
    layer_kernel(nc, aps, y)
    return run(nc, [arrays], core_ids=[0]).results[0]["out_y"]
```

```python
import numpy as np

import concourse.bass as bass
from concourse import mybir
from contextlib import ExitStack

F32 = mybir.dt.float32
F32R = mybir.dt.float32r
ALU = mybir.AluOpType
ACT = mybir.ActivationFunctionType
AX = mybir.AxisListType

D, S, DFF = 1024, 512, 4096
P = 128
NT = S // P
KD = D // P
KF = DFF // P
HEADS, NOPE, ROPE, VD = 8, 64, 32, 64
QK = NOPE + ROPE
HALF = ROPE // 2
QL, KVL = 384, 256
NQL, NKVL = QL // P, KVL // P
NLORA = NQL + NKVL
DW = HEADS * 64
C_DIL = QL + KVL + ROPE
C_GATE = C_DIL + 3 * DW
LN_EPS, RMS_EPS = 1e-5, 1e-6
NEG = -1e30
ALPHA = 2.0 ** 0.25
MLA_SCALE = QK ** -0.5
DIL_SCALE = 64 ** -0.5
SLOPES = [2.0 ** (-8.0 * (i + 1) / HEADS) for i in range(HEADS)]
PATTERNS = ((128, 1), (512, 4), (2048, 16))

K_ID, K_CAUSAL, K_COS, K_SIN, K_DIST, K_COUNT = 0, P, 2 * P, 2 * P + NT * HALF, 2 * P + 2 * NT * HALF, 2 * P + 2 * NT * HALF + S
K_ALL = K_COUNT + S
SMALL = K_DIST


def constants():
    t = np.zeros((P, K_ALL), np.float32)
    t[:, K_ID:K_ID + P] = np.eye(P)
    row, col = np.arange(P)[:, None], np.arange(P)[None, :]
    t[:, K_CAUSAL:K_CAUSAL + P] = np.where(col <= row, 0.0, NEG)
    inv = np.power(np.float32(10000.0), -np.arange(HALF, dtype=np.float32) / np.float32(HALF)).astype(np.float32)
    pos = (np.arange(NT)[None, :] * P + np.arange(P)[:, None]).astype(np.float32)
    ang = (pos[:, :, None] * inv[None, None, :]).astype(np.float32)
    t[:, K_COS:K_COS + NT * HALF] = np.cos(ang).reshape(P, -1)
    t[:, K_SIN:K_SIN + NT * HALF] = np.sin(ang).reshape(P, -1)
    dist = (S - P) + np.arange(P)[:, None] - np.arange(S)[None, :]
    count = np.zeros((P, S))
    for window, dilation in PATTERNS:
        count += (dist >= 0) & (dist % dilation == 0) & (dist <= window)
    t[:, K_DIST:K_DIST + S] = -dist
    t[:, K_COUNT:K_COUNT + S] = np.where(count > 0, np.log(np.maximum(count, 1)), NEG)
    return t


NPROJ = 3 * (DW // P) + 2 * KD
PRE = 2
UNITS = [("lora", m) for m in range(3)]
for _k in range(NQL):
    UNITS += [("lora", _k + 3), ("uq", _k)]
UNITS += [("proj", p) for p in range(3)] + [("ukv", k) for k in range(NKVL)] + [("proj", p) for p in range(3, NPROJ)]
UNITS += [("y", 0), ("y", 1), ("y", 2)]
for _m in range(5):
    UNITS += [("y", _m + 3), ("out", _m)]
UNITS += [("out", _m) for _m in range(5, KD)]
UNITS += [("ff1", m) for m in range(KF)] + [("ff2", 0), ("ff2", 1), ("ff2", 2)]
LAST = 8
for _k in range(KF - LAST):
    if _k + 3 < KF - LAST:
        UNITS += [("ff2", _k + 3)]
    if _k % 3 == 2:
        UNITS += [("ff2", KF - LAST + _k // 3)]
POS = {u: n for n, u in enumerate(UNITS)}
IN_RING = [u for u in UNITS if not (u[0] in ("uq", "ukv", "out") or (u[0] == "ff2" and u[1] >= KF - LAST))]
RING = {u: n for n, u in enumerate(IN_RING)}
NRAW = NRING = 3
POOLED = [u for u in UNITS if u[0] in ("uq", "ukv") or (u[0] == "proj" and u[1] > PRE + 2 and (u[1] - PRE) % 3 != 1)]
LOW_COUNT, _low = {}, [0, 0]
for _u in UNITS:
    _low[_u in POOLED] += 1
    LOW_COUNT[_u] = _low[_u in POOLED]
FF1_ROUNDS = KF // 3
IN_LOOP = [("ff1", m) for m in range(3, 3 * FF1_ROUNDS)]
WIDTH = {u: (HEADS * QK if u[0] == "uq" else 1024) for u in UNITS}
WIDTH[("lora", NLORA)] = KD * ROPE
RAW_COUNT = {}
_count = [0] * NRAW
for _n, _u in enumerate(UNITS):
    _count[_n % NRAW] += 32 if _u[0] == "y" else 16
    RAW_COUNT[_u] = _count[_n % NRAW]

TEVENTS = [("q", 0), ("k", 0)]
for _g in range(2 * HEADS):
    if _g + 1 < HEADS:
        TEVENTS += [("q", _g + 1), ("k", _g + 1)]
    if _g >= HEADS and _g % 2 == 0:
        TEVENTS += [("v", _g)]
    TEVENTS += [("p0", _g), ("p1", _g), ("p2", _g)]
TBANK = {"q": 0, "k": 1, "v": 1, "p0": 0, "p1": 1, "p2": 0}
TI = {e: n for n, e in enumerate(TEVENTS)}
TPREV = {}
_lastof = {0: None, 1: None}
for _e in TEVENTS:
    TPREV[_e] = _lastof[TBANK[_e[0]]]
    _lastof[TBANK[_e[0]]] = TI[_e]

SPLACE = {3: (0, 0), 2: (1, 0), 1: (2, 0), 0: (2, 256)}
SORDER = [(0, (3,)), (1, (2,)), (2, (1, 0))]
POFF = {0: 0, 1: 128, 2: 384, 3: 768}
KOFF = {0: 0, 1: 512, 2: 896, 3: 1152}
PW = 1280


def layer_kernel(nc, a, out):
    st, sx, sb_, sc_ = ExitStack(), ExitStack(), ExitStack(), ExitStack()
    with st:
        def sb(name, shape, dt=F32, stack=st):
            return stack.enter_context(nc.sbuf_tensor(name, shape, dt))

        def sem(name):
            return st.enter_context(nc.semaphore(name))

        ring_h = sb("ring_high", [P, NRING, 1024], F32R)
        ring_l = sb("ring_low", [P, NRING, 1024], F32R)
        raw = sb("raw_weights", [P, NRAW, 1024])
        tab = sb("tables", [P, 2048])
        small = sb("small_constants", [P, SMALL])
        ones = sb("ones", [P, P], F32R)
        krot = sb("k_rotary", [P, NT, ROPE])
        gq = sb("g_lora", [P, NLORA])
        bg = sb("b_gate_columns", [P, 2 * KD])
        epss = sb("eps", [P, 2])
        mx = sb("row_max", [P, NT])
        nm = sb("minus_max", [P, NT])
        rs = sb("row_sum", [P, NT])
        rr = sb("row_sum_inverse", [P, NT])
        bns = sb("bn_statistics", [P, NT, 2, 6])
        mv = sb("mean_variance", [P, NT, 2])
        std = sb("deviation", [P, NT])
        rstd = sb("deviation_inverse", [P, NT])

        xt = sb("x_transposed", [P, KD, 2, S], F32R, sx)
        ot = sb("o_transposed", [P, HEADS, 2, S], F32R, sb_)
        att = sb("attention_buffers", [P, 8192], F32R, sb_)
        tok = sb("token_major", [P, 8192], F32, sb_)
        dilf = sb("dilated_qkv", [P, 3, 4, S], F32, sc_)
        pbuf = sb("probabilities", [P, 2048], F32, sc_)
        sc_.close()
        mixed = sb("mixed_transposed", [P, KD, 2, S], F32R, sb_)
        sb_.close()
        sx.close()
        tail = sb("h_residual", [P, 2, 4096])
        ff = sb("hidden_transposed", [P, KF, 2, S], F32R)

        bank = [st.enter_context(nc.psum_tensor(f"bank{n}", [P, 512], F32)) for n in range(8)]
        SB, TB, OB = bank[2:5], bank[5:7], bank[7]

        ident, causal = small[:, K_ID:K_ID + P], small[:, K_CAUSAL:K_CAUSAL + P]
        cos = small[:, K_COS:K_COS + NT * HALF].rearrange("p (t i) -> p t i", t=NT)
        sin = small[:, K_SIN:K_SIN + NT * HALF].rearrange("p (t i) -> p t i", t=NT)
        ptb = att[:, 0:2 * PW].rearrange("p (s n) -> p s n", s=2)
        qkb = att[:, 2560:6656].rearrange("p (b q s n) -> p b q s n", b=2, q=2, s=2)
        ukv = att[:, 2560:6656].rearrange("p (k s n) -> p k s n", k=2, s=2)
        uqb = [ot[:, 5:8, :, :].rearrange("p k s n -> p (k s n)")[:, n * 1536:(n + 1) * 1536] for n in range(2)] + [att[:, 0:1536]]
        uq = [b.rearrange("p (s n) -> p s n", s=2) for b in uqb]
        vb = att[:, 6656:7680].rearrange("p (t c s d) -> p t c s d", t=NT, c=2, s=2)
        ofold = pbuf[:, PW:PW + S]
        lora = ot[:, 0:NLORA, :, :]
        xtok = tok[:, 0:4096].rearrange("p (t n) -> p t n", t=NT)
        hres = tok[:, 4096:8192].rearrange("p (t n) -> p t n", t=NT)
        qf = tok[:, 0:3072].rearrange("p (t h d) -> p t h d", t=NT, h=HEADS)
        kf = tok[:, 3072:6144].rearrange("p (t h d) -> p t h d", t=NT, h=HEADS)
        vf = tok[:, 6144:8192].rearrange("p (t h d) -> p t h d", t=NT, h=HEADS)
        z = tok[:, :].rearrange("p (m n) -> p m n", m=2 * KD)
        flat = dilf[:, :, :, :].rearrange("p c j n -> p (c j n)")
        lraw = flat[:, 0:NLORA * S].rearrange("p (m n) -> p m n", m=NLORA)
        krt = flat[0:2 * ROPE, 2560:3072]
        rinv = flat[:, 3072:4096].rearrange("p (c n) -> p c n", c=2)
        ltmp = flat[:, 4096:5120].rearrange("p (c n) -> p c n", c=2)
        sqt = pbuf[:, 0:1024].rearrange("p (c n) -> p c n", c=2)
        sqh = qkb[:, :, :, :, :].rearrange("p b q s n -> p (b q) s n")
        rtmp = pbuf[:, 1024:1536].rearrange("p (a h i) -> p a h i", a=4, h=HEADS)
        wout = [xt, att[:, :].rearrange("p (k s n) -> p k s n", k=KD, s=2)]
        dist, lcount = tab[:, 0:S], tab[:, S:2 * S]
        bias = tab[:, 2 * S:4 * S].rearrange("p (b n) -> p b n", b=2)
        lng, lnb = tab[:, 0:D], tab[:, D:2 * D]
        relu = tab[:, 0:1536].rearrange("p (b n) -> p b n", b=3)
        fsq = tab[:, 1536:2048]
        h2 = tail[:, 0, :].rearrange("p (t n) -> p t n", t=NT)

        spill = nc.dram_tensor("h_spill", (S, D), F32).ap().rearrange("(t p) n -> p t n", p=P)

        raw_in = [sem(f"raw_in{n}") for n in range(NRAW)]
        x_in, const_in, small_in = [sem(f"x_in{n}") for n in range(2)], sem("const_in"), sem("small_in")
        w_high = sem("w_high")
        w_low, w_low_pool = sem("w_low"), sem("w_low_pool")
        unit_done = sem("unit_done")
        xt_ps, xt_high, xt_low = sem("xt_ps"), sem("xt_high"), sem("xt_low")
        acc_read = sem("acc_read")
        ones_set, eps_set = sem("ones_set"), sem("eps_set")
        sq_high, sq_low, sum_ps, dev_set, inv_set = sem("sq_high"), sem("sq_low"), sem("sum_ps"), sem("dev_set"), sem("inv_set")
        norm_set, norm_high, norm_low = sem("norm_set"), sem("norm_high"), sem("norm_low")
        krt_ps, krot_set, krot_spread = sem("krt_ps"), sem("krot_set"), sem("krot_spread")
        qkv_ps, qkv_read, q_rot, ukv_done = sem("qkv_ps"), sem("qkv_read"), sem("q_rot"), sem("ukv_done")
        t_ps, t_high, t_low = sem("t_ps"), sem("t_high"), sem("t_low")
        sc_ps, max_set, exp_set, p_set = sem("scores_ps"), sem("max_set"), sem("exp_set"), sem("p_set")
        v_high, v_low, qk_high, qk_low = sem("v_high"), sem("v_low"), sem("qk_high"), sem("qk_low")
        pv_ps, o_fold, o_sum, o_high, o_low, bias_set = sem("pv_ps"), sem("o_fold"), sem("o_sum"), sem("o_high"), sem("o_low"), sem("bias_set")
        gate_set, mix_read, mix_set, mix_high, mix_low = sem("gate_set"), sem("mix_read"), sem("mix_set"), sem("mix_high"), sem("mix_low")
        out_ps, res_set, x2_in, ln_in, var_set, dev1_set = sem("out_ps"), sem("res_set"), [sem(f"x2_in{t}") for t in range(NT)], sem("ln_in"), sem("var_set"), sem("dev1_set")
        h_set, ht_ps, ht_high, ht_low, spilled = sem("h_set"), sem("ht_ps"), sem("ht_high"), sem("ht_low"), sem("spilled")
        relu_set, fsq_set, f_high, f_low = sem("relu_set"), sem("fsq_set"), sem("f_high"), sem("f_low")
        h2_in, ln2_in, ff2_ps, var2_set, dev2_set, y_set, out_done = sem("h2_in"), sem("ln2_in"), sem("ff2_ps"), sem("var2_set"), sem("dev2_set"), sem("y_set"), sem("out_done")
        dchain, pchain = sem("vector_chain"), sem("pool_chain")

        cols = lambda w: w.rearrange("(k p) n -> p k n", p=P)
        w_in, w_ff1, w_a, w_b = cols(a["w_in"][0]), cols(a["w_ff1"][0]), cols(a["w_o_mla"][0]), cols(a["w_o_dil"][0])

        def unit_source(u):
            kind, n = u
            if kind == "lora":
                return [(0, KD, w_in[:, :, n * P:min((n + 1) * P, C_DIL)])]
            if kind == "uq":
                return [(0, None, a["w_uq"][0][n * P:(n + 1) * P, :])]
            if kind == "ukv":
                return [(0, None, a["w_ukv"][0][n * P:(n + 1) * P, :])]
            if kind == "proj":
                c = C_DIL + (n % 3) * DW + (n // 3) * P if n < 12 else C_GATE + (n - 12) * P
                return [(0, KD, w_in[:, :, c:c + P])]
            if kind == "y":
                return [(0, 4, w_a[:, :, n * P:(n + 1) * P]), (512, 4, w_b[:, :, n * P:(n + 1) * P])]
            if kind == "out":
                return [(0, None, a["w_out"][0][n * P:(n + 1) * P, :])]
            if kind == "ff1":
                return [(0, KD, w_ff1[:, :, n * P:(n + 1) * P])]
            return [(0, None, a["w_ff2"][0][n * P:(n + 1) * P, :])]

        def wait_split(eng, u):
            eng.wait_ge(w_low_pool if u in POOLED else w_low, LOW_COUNT[u])

        def split_dest(u):
            src = raw[:, POS[u] % NRAW, 0:WIDTH[u]]
            kind, n = u
            if kind == "uq":
                return src, uq[n][:, 0, :], uq[n][:, 1, :]
            if kind == "ukv":
                return src, ukv[:, n, 0, :], ukv[:, n, 1, :]
            if kind == "ff2" and n >= KF - LAST:
                j = n - (KF - LAST)
                return src, ff[:, 2 * j, :, :].rearrange("p s n -> p (s n)"), ff[:, 2 * j + 1, :, :].rearrange("p s n -> p (s n)")
            if kind == "out":
                return src, None, None
            slot = RING[u] % NRING
            if u == ("lora", NLORA):
                both = ring_h[:, slot, 0:2 * KD * ROPE].rearrange("p (k s n) -> p k s n", k=KD, s=2)
                return src.rearrange("p (k n) -> p k n", k=KD), both[:, :, 0, :], both[:, :, 1, :]
            return src, ring_h[:, slot, 0:WIDTH[u]], ring_l[:, slot, 0:WIDTH[u]]

        block = st.enter_context(nc.Block())

        @block.sync
        def _(sp):
            def load_x(n):
                half = slice(n * S, (n + 1) * S)
                sp.dma_start(xtok[:, :, half], a["x"][0].rearrange("(t p) n -> p t n", p=P)[:, :, half]).then_inc(x_in[n], 16)

            sp.dma_start(small[:, :], a["const"][:, 0:SMALL]).then_inc(small_in, 16)
            load_x(0)
            for n, u in enumerate(UNITS):
                if u == IN_LOOP[0]:
                    with sp.Fori(1, FF1_ROUNDS) as i:
                        for b in range(3):
                            ff1_slot = POS[("ff1", b)] % NRAW
                            sp.wait_ge(w_low, 3 * i + (LOW_COUNT[("ff1", b)] - 3))
                            sp.dma_start(raw[:, ff1_slot, :].rearrange("p (k n) -> p k n", k=KD),
                                         w_ff1[:, :, bass.ds((3 * i + b) * P, P)]).then_inc(raw_in[ff1_slot], 16)
                if u in IN_LOOP:
                    continue
                slot = n % NRAW
                if n >= NRAW:
                    wait_split(sp, UNITS[n - NRAW])
                for first, tiles, src in unit_source(u):
                    dst = raw[:, slot, first:first + (512 if u[0] == "y" else WIDTH[u])]
                    if tiles:
                        dst = dst.rearrange("p (k n) -> p k n", k=tiles)
                    sp.dma_start(dst, src).then_inc(raw_in[slot], 16)
                if n == 0:
                    load_x(1)
                if n == 2:
                    with nc.allow_non_contiguous_dma(reason="one small column per lora tile"):
                        sp.dma_start(gq[:, 0:NQL], a["g_q_a"][0].rearrange("(m p) -> p m", p=P)).then_inc(const_in, 16)
                        sp.dma_start(gq[:, NQL:NLORA], a["g_kv_a"][0].rearrange("(m p) -> p m", p=P)).then_inc(const_in, 16)
                        sp.dma_start(bg[:, :], a["b_gate"][0].rearrange("b (m p) -> p (b m)", p=P)).then_inc(const_in, 16)
                    sp.dma_start(tab[:, 0:2 * S], a["const"][:, K_DIST:K_ALL]).then_inc(const_in, 16)
            for t in range(NT):
                for n in range(2) if t == NT - 1 else (slice(None),):
                    half = slice(n * S, (n + 1) * S) if t == NT - 1 else n
                    sp.wait_ge(y_set, t + 1 + (n if t == NT - 1 else 0))
                    sp.dma_start(out[0][t * P:(t + 1) * P, half], h2[:, t, half]).then_inc(out_done, 16)
            sp.wait_ge(out_done, 16 * (NT + 1))

        @block.gpsimd
        def _(pool):
            nc.gpsimd.memset(epss[:, 0:1], RMS_EPS).then_inc(eps_set, 1)
            nc.gpsimd.memset(epss[:, 1:2], LN_EPS).then_inc(eps_set, 1)
            def prep(u):
                src, high, lo = split_dest(u)
                pool.wait_ge(w_high, POS[u] + 1)
                nc.gpsimd.tensor_tensor(lo, src, high.bitcast(F32), ALU.subtract).then_inc(w_low_pool, 1)

            for k in range(NQL):
                prep(("uq", k))
            for t in range(NT):
                if t == 0:
                    pool.wait_ge(krot_set, 2)
                    pool.wait_ge(xt_low, KD)
                    pool.wait_ge(xt_high, KD)
                nc.gpsimd.tensor_copy(kf[:, t, :, NOPE:QK],
                                      krot[:, t, :].unsqueeze(1).broadcast_to([P, HEADS, ROPE])).then_inc(krot_spread, 1)
            for k in range(NKVL):
                prep(("ukv", k))
            pool.wait_ge(const_in, 64)

            def dilated_bias(h):
                if h >= 2:
                    pool.wait_ge(max_set, 3 * (HEADS + h - 1))
                nc.gpsimd.tensor_scalar(bias[:, h % 2, :], dist, SLOPES[h], None, ALU.mult).then_inc(pchain, 1)
                pool.wait_ge(pchain, h + 1)
                nc.gpsimd.tensor_tensor(bias[:, h % 2, :], bias[:, h % 2, :], lcount, ALU.add).then_inc(bias_set, 1)

            dilated_bias(0)
            dilated_bias(1)
            for g in range(2 * HEADS):
                if HEADS <= g < 2 * HEADS - 2:
                    dilated_bias(g - HEADS + 2)
                for p in (PRE + (3 * g) // 2, PRE + 1 + (3 * g) // 2)[:1 + g % 2]:
                    if ("proj", p + 3) in POOLED:
                        prep(("proj", p + 3))
            pool.wait_ge(bias_set, HEADS)
            pool.wait_ge(max_set, 6 * HEADS)
            pool.dma_start(lng, a["ln1_g"].broadcast_to([P, D])).then_inc(ln_in, 16)
            pool.dma_start(lnb, a["ln1_b"].broadcast_to([P, D])).then_inc(ln_in, 16)
            pool.wait_ge(mix_low, KD)
            for t in range(NT):
                pool.dma_start(xtok[:, t, :], a["x"][0][t * P:(t + 1) * P, :]).then_inc(x2_in[t], 16)
            for t in range(NT):
                pool.wait_ge(h_set, t + 1)
                pool.dma_start(spill[:, t, :], hres[:, t, :]).then_inc(spilled, 16)
            pool.wait_ge(f_low, KF)
            pool.wait_ge(spilled, 16 * NT)
            pool.dma_start(h2, spill).then_inc(h2_in, 16)
            pool.dma_start(lng, a["ln2_g"].broadcast_to([P, D])).then_inc(ln2_in, 16)
            pool.dma_start(lnb, a["ln2_b"].broadcast_to([P, D])).then_inc(ln2_in, 16)

        @block.scalar
        def _(act):
            copy = ACT.Copy

            def prep(u):
                src, high, _ = split_dest(u)
                act.wait_ge(raw_in[POS[u] % NRAW], RAW_COUNT[u])
                if u in RING and RING[u] >= NRING:
                    act.wait_ge(unit_done, RING[u] - NRING + 1)
                if u[0] == "out":
                    if u[1] == 0:
                        act.wait_ge(unit_done, RING[("proj", NPROJ - 1)] + 1)
                        act.wait_ge(pv_ps, 2 * HEADS)
                    nc.scalar.activation(wout[0][:, u[1], 0, :], src[:, 0:S], copy)
                    nc.scalar.activation(wout[1][:, u[1], 0, :], src[:, S:D], copy).then_inc(w_high, 1)
                    return
                if u[0] == "ff2" and u[1] >= KF - LAST:
                    j = u[1] - (KF - LAST)
                    act.wait_ge(unit_done, RING[("ff2", 2 * j + 1)] + 1)
                nc.scalar.activation(high, src, copy).then_inc(w_high, 1)

            for k in range(KD):
                act.wait_ge(xt_ps, k + 1)
                nc.scalar.activation(xt[:, k, 0, :], bank[2 + k % 6][:, :], copy).then_inc(xt_high, 1)
                if k in (0, 4, 7):
                    prep(UNITS[(0, 4, 7).index(k)])

            def norm_deviation(c):
                act.wait_ge(sum_ps, c + 1)
                act.wait_ge(eps_set, 2)
                nc.scalar.activation(rinv[:, c, :], bank[6 + c][:, :], ACT.Sqrt, bias=epss[:, 0:1],
                                     scale=1.0 / (QL, KVL)[c]).then_inc(dev_set, 1)

            def norm_high_parts(c):
                for m in (range(NQL), range(NQL, NLORA))[c]:
                    act.wait_ge(norm_set, m + 1)
                    nc.scalar.activation(lora[:, m, 0, :], ltmp[:, m % 2, :], copy).then_inc(norm_high, 1)

            act.wait_ge(xt_low, KD)
            for m in range(NLORA + 1):
                act.wait_ge(unit_done, m + 1)
                ps = bank[m % 2]
                if m < NLORA:
                    nc.scalar.activation(lraw[:, m, :], ps[:, :], copy).then_inc(acc_read, 1)
                    act.wait_ge(acc_read, m + 1)
                    if m >= 4:
                        act.wait_ge(sum_ps, 1)
                    nc.scalar.activation(sqh[:, m % 4, 0, :], lraw[:, m, :], ACT.Square).then_inc(sq_high, 1)
                else:
                    nc.scalar.activation(krt, ps[0:2 * ROPE, :], copy).then_inc(acc_read, 1)
                prep(IN_RING[m + 3])
                if m < NQL:
                    prep(("uq", m))
                if m == NQL - 1:
                    norm_deviation(0)
                if m == NQL:
                    norm_high_parts(0)

            def unit_event(p):
                act.wait_ge(unit_done, RING[("proj", p)] + 1)
                ps = bank[(NLORA + 1 + p) % 2][:, :]
                if p < 12:
                    nc.scalar.activation(dilf[:, p % 3, p // 3, :], ps, copy).then_inc(acc_read, 1)
                else:
                    nc.scalar.activation(z[:, p - 12, :], ps, ACT.Identity, bias=bg[:, p - 12:p - 11]).then_inc(acc_read, 1)
                prep(IN_RING[RING[("proj", p)] + 3])

            norm_deviation(1)
            norm_high_parts(1)
            act.wait_ge(sum_ps, 2)
            act.wait_ge(sq_low, NLORA)
            prep(("ukv", 0))
            prep(("ukv", 1))
            for i in range(4 * NT):
                t, c, b = (i % 8) // 2, i % 2, 2 + i % 6
                act.wait_ge(qkv_ps, i + 1)
                if i < 8:
                    nc.scalar.activation(qf[:, t, 4 * c:4 * c + 4, :],
                                         bank[b][:, 0:384].rearrange("p (h d) -> p h d", h=4), copy).then_inc(qkv_read, 1)
                else:
                    ps = bank[b][:, :].rearrange("p (h d) -> p h d", h=4)
                    nc.scalar.activation(kf[:, t, 4 * c:4 * c + 4, 0:NOPE], ps[:, :, 0:NOPE], copy)
                    nc.scalar.activation(vf[:, t, 4 * c:4 * c + 4, :], ps[:, :, NOPE:NOPE + VD], copy).then_inc(qkv_read, 1)

            def transposed(kind, g):
                i = TI[(kind, g)]
                ps = TB[TBANK[kind]]
                act.wait_ge(t_ps, i + 1)
                if kind in ("q", "k"):
                    dst, src = qkb[0:QK, g % 2, "qk".index(kind), 0, :], ps[0:QK, :]
                elif kind == "v":
                    dst = vb[:, :, :, 0, :]
                    src = ps[:, :].rearrange("p (t c d) -> p t c d", t=NT, c=2)
                else:
                    o, w = {"p0": (0, 512), "p1": (512, 384), "p2": (896, 384)}[kind]
                    dst, src = ptb[:, 0, o:o + w], ps[:, 0:w]
                nc.scalar.activation(dst, src, copy).then_inc(t_high, 1)

            transposed("q", 0)
            transposed("k", 0)
            for p in range(PRE):
                unit_event(p)

            def output_fold(g):
                c = g % 2
                act.wait_ge(pv_ps, g + 1)
                if g:
                    act.wait_ge(o_low, g)
                nc.scalar.activation(ofold[64 - 64 * c:128 - 64 * c, :], OB[64:128, :], copy).then_inc(o_fold, 1)

            def output_high(g):
                rows = slice(64 * (g % 2), 64 * (g % 2) + 64)
                act.wait_ge(o_sum, g + 1)
                nc.scalar.activation(ot[rows, g // 2, 0, :], ofold[rows, :], copy).then_inc(o_high, 1)

            for g in range(2 * HEADS):
                if g:
                    output_fold(g - 1)
                if g % 2 == 0 and g < HEADS:
                    act.wait_ge(qkv_read, 4 * NT)
                    nc.scalar.activation(vb[:, :, :, 0, :], vf[:, :, g:g + 2, :], copy).then_inc(v_high, 1)
                if g + 1 < HEADS:
                    transposed("q", g + 1)
                    transposed("k", g + 1)
                if g >= HEADS and g % 2 == 0:
                    transposed("v", g)
                for n, (b, blocks) in enumerate(SORDER):
                    act.wait_ge(max_set, 3 * g + n + 1)
                    for qb in blocks:
                        o, w = SPLACE[qb][1], P * (qb + 1)
                        p = pbuf[:, POFF[qb]:POFF[qb] + w]
                        src, scale = (SB[b][:, o:o + w], MLA_SCALE) if g < HEADS else (p, 1.0)
                        nc.scalar.activation(p, src, ACT.Exp, bias=nm[:, qb:qb + 1], scale=scale,
                                             accum_out=rs[:, qb:qb + 1]).then_inc(exp_set, 1)
                if g >= HEADS - 1 and g % 2 == 1 and g < 2 * HEADS - 1:
                    j = (g - HEADS + 1) // 2
                    act.wait_ge(acc_read, NLORA + 1 + 3 * j + 3)
                    nc.scalar.activation(qkb[:, j % 2, :, 0, :], dilf[:, 0:2, j, :], copy).then_inc(qk_high, 1)
                if g % 2 == 1:
                    unit_event(PRE + (3 * g) // 2)
                transposed("p0", g)
                transposed("p1", g)
                if g:
                    output_high(g - 1)
                transposed("p2", g)
                unit_event(PRE + g + (g + 1) // 2)
            output_fold(2 * HEADS - 1)
            output_high(2 * HEADS - 1)
            for p in range(PRE + 3 * HEADS, NPROJ):
                unit_event(p)

            act.wait_ge(acc_read, NLORA + 1 + NPROJ)
            for m in range(KD):
                for b in range(2):
                    nc.scalar.activation(z[:, b * KD + m, :], z[:, b * KD + m, :], ACT.Sigmoid).then_inc(gate_set, 1)
                act.wait_ge(unit_done, RING[("y", m)] + 1)
                if m + 3 < KD:
                    prep(("y", m + 3))
                prep(("out", m))
                act.wait_ge(mix_set, m + 1)
                nc.scalar.activation(mixed[:, m, 0, :], z[:, m, :], copy).then_inc(mix_high, 1)
            for m in range(3):
                prep(("ff1", m))

            def deviation(t):
                act.wait_ge(var_set, t + 1)
                nc.scalar.activation(std[:, t:t + 1], mv[:, t, 1:2], ACT.Sqrt, bias=epss[:, 1:2]).then_inc(dev1_set, 1)

            deviation(0)
            deviation(1)
            for t in range(NT):
                for c in range(2):
                    act.wait_ge(ht_ps, 2 * t + c + 1)
                    nc.scalar.activation(xt[:, 4 * c:4 * c + 4, 0, t * P:(t + 1) * P],
                                         bank[4 + 2 * (t % 2) + c][:, :].rearrange("p (k n) -> p k n", k=4),
                                         copy).then_inc(ht_high, 1)
                if t + 2 < NT:
                    deviation(t + 2)

            def squared_relu(i, b):
                unit = ("ff1", b)
                act.wait_ge(unit_done, 3 * i + (RING[unit] + 1))
                nc.scalar.activation(relu[:, b, :], bank[b][:, :], ACT.Relu).then_inc(relu_set, 1)
                act.wait_ge(relu_set, 3 * i + (b + 1))
                nc.scalar.activation(ff[:, 3 * i + b, 0, :], relu[:, b, :], ACT.Square).then_inc(f_high, 1)
                src, high, _ = split_dest(unit)
                act.wait_ge(raw_in[POS[unit] % NRAW], 16 * i + (RAW_COUNT[unit] + 16))
                nc.scalar.activation(high, src, copy).then_inc(w_high, 1)

            act.wait_ge(h_set, NT)
            for b in range(3):
                squared_relu(0, b)
            act.wait_ge(spilled, 16 * NT)
            with act.Fori(1, FF1_ROUNDS) as i:
                for b in range(3):
                    act.wait_ge(f_low, 3 * i + (b - 2))
                    squared_relu(i, b)
            for b in range(KF - 3 * FF1_ROUNDS):
                act.wait_ge(f_low, 3 * FF1_ROUNDS + (b - 2))
                squared_relu(FF1_ROUNDS, b)
            for k in range(KF - LAST):
                if k + 3 < KF - LAST:
                    prep(("ff2", k + 3))
                if k % 3 == 2:
                    prep(("ff2", KF - LAST + k // 3))
            for t in range(NT):
                act.wait_ge(var2_set, t + 1)
                nc.scalar.activation(std[:, t:t + 1], mv[:, t, 1:2], ACT.Sqrt, bias=epss[:, 1:2]).then_inc(dev2_set, 1)

        @block.vector
        def _(dve):
            links = [0]

            def link(ins):
                links[0] += 1
                ins.then_inc(dchain, 1)
                dve.wait_ge(dchain, links[0])

            def low(dst, src, high, done):
                nc.vector.tensor_tensor(dst, src, high.bitcast(F32), ALU.subtract).then_inc(done, 1)

            def prep(u):
                if u in POOLED:
                    return
                src, high, lo = split_dest(u)
                dve.wait_ge(w_high, POS[u] + 1)
                if u[0] == "out":
                    for n in range(2):
                        ins = nc.vector.tensor_tensor(wout[n][:, u[1], 1, :], src[:, n * S:(n + 1) * S],
                                                      wout[n][:, u[1], 0, :].bitcast(F32), ALU.subtract)
                    ins.then_inc(w_low, 1)
                    return
                low(lo, src, high, w_low)

            nc.vector.memset(ones[:, :].bitcast(F32), 1.0).then_inc(ones_set, 1)
            for k in range(KD):
                dve.wait_ge(xt_high, k + 1)
                low(xt[:, k, 1, :], bank[2 + k % 6][:, :], xt[:, k, 0, :], xt_low)
                if k in (0, 4, 7):
                    prep(UNITS[(0, 4, 7).index(k)])

            def norm_inverse(c):
                dve.wait_ge(dev_set, c + 1)
                link(nc.vector.reciprocal(rinv[:, c, :], rinv[:, c, :]))

            def norm(c):
                dve.wait_ge(const_in, 64)
                tiles = (range(NQL), range(NQL, NLORA))[c]

                def scaled(m):
                    if m >= 2:
                        dve.wait_ge(norm_low, m - 1)
                    nc.vector.scalar_tensor_tensor(out=ltmp[:, m % 2, :], in0=lraw[:, m, :], scalar=gq[:, m:m + 1],
                                                   in1=rinv[:, c, :], op0=ALU.mult, op1=ALU.mult).then_inc(norm_set, 1)

                scaled(tiles[0])
                for m in tiles:
                    if m + 1 in tiles:
                        scaled(m + 1)
                    dve.wait_ge(norm_high, m + 1)
                    low(lora[:, m, 1, :], ltmp[:, m % 2, :], lora[:, m, 0, :], norm_low)

            for m in range(NLORA + 1):
                if m < NLORA:
                    dve.wait_ge(acc_read, m + 1)
                    if m >= 2:
                        dve.wait_ge(sq_low, m - 1)
                    link(nc.vector.tensor_tensor(sqt[:, m % 2, :], lraw[:, m, :], lraw[:, m, :], ALU.mult))
                    dve.wait_ge(sq_high, m + 1)
                    low(sqh[:, m % 4, 1, :], sqt[:, m % 2, :], sqh[:, m % 4, 0, :], sq_low)
                prep(IN_RING[m + 3])
                if m < NQL:
                    prep(("uq", m))
                if m == NQL - 1:
                    norm_inverse(0)
                if m == NQL:
                    norm(0)

            def rotate(lo_out, hi_out, t1, t2, c, s):
                shape = [P] + list(t1.shape[1:])
                prod = [rtmp[:, n, :, :] if len(shape) == 3 and shape[1] == HEADS else
                        pbuf[:, 1536 + n * NT * HALF:1536 + (n + 1) * NT * HALF].rearrange("p (t i) -> p t i", t=NT)
                        for n in range(4)]
                nc.vector.tensor_tensor(prod[0], t1, c, ALU.mult)
                nc.vector.tensor_tensor(prod[1], t2, s, ALU.mult)
                nc.vector.tensor_tensor(prod[2], t1, s, ALU.mult)
                link(nc.vector.tensor_tensor(prod[3], t2, c, ALU.mult))
                nc.vector.tensor_tensor(lo_out, prod[0], prod[1], ALU.subtract)
                return nc.vector.tensor_tensor(hi_out, prod[2], prod[3], ALU.add)

            def unit_event(p):
                prep(IN_RING[RING[("proj", p)] + 3])

            dve.wait_ge(krt_ps, 1)
            dve.wait_ge(small_in, 16)
            kps = bank[5][:, 0:2 * NT * ROPE].rearrange("p (t s d) -> p s t d", t=NT, s=2)
            k1, k2 = krot[:, :, 0:HALF], krot[:, :, HALF:ROPE]
            link(nc.vector.tensor_copy(krot[:, :, :], kps[:, 0, :, :]))
            link(nc.vector.tensor_tensor(krot[:, :, :], krot[:, :, :], kps[:, 1, :, :], ALU.add))
            rotate(k1, k2, k1, k2, cos, sin).then_inc(krot_set, 2)
            norm_inverse(1)
            norm(1)
            prep(("ukv", 0))
            prep(("ukv", 1))
            for t in range(NT):
                dve.wait_ge(qkv_read, 2 * t + 2)
                if t:
                    dve.wait_ge(q_rot, t)
                q1, q2 = qf[:, t, :, NOPE:NOPE + HALF], qf[:, t, :, NOPE + HALF:QK]
                rotate(q1, q2, q1, q2, cos[:, t, :].unsqueeze(1).broadcast_to([P, HEADS, HALF]),
                       sin[:, t, :].unsqueeze(1).broadcast_to([P, HEADS, HALF])).then_inc(q_rot, 1)

            def transposed(kind, g):
                i = TI[(kind, g)]
                ps = TB[TBANK[kind]]
                dve.wait_ge(t_high, i + 1)
                if kind in ("q", "k"):
                    b = qkb[0:QK, g % 2, "qk".index(kind), :, :]
                    low(b[:, 1, :], ps[0:QK, :], b[:, 0, :], t_low)
                elif kind == "v":
                    low(vb[:, :, :, 1, :], ps[:, :].rearrange("p (t c d) -> p t c d", t=NT, c=2), vb[:, :, :, 0, :], t_low)
                else:
                    o, w = {"p0": (0, 512), "p1": (512, 384), "p2": (896, 384)}[kind]
                    low(ptb[:, 1, o:o + w], ps[:, 0:w], ptb[:, 0, o:o + w], t_low)

            transposed("q", 0)
            transposed("k", 0)
            for p in range(PRE):
                unit_event(p)

            def output_sum(g):
                mine, other = slice(64 * (g % 2), 64 * (g % 2) + 64), slice(64 - 64 * (g % 2), 128 - 64 * (g % 2))
                dve.wait_ge(o_fold, g + 1)
                nc.vector.tensor_tensor(ofold[mine, :], OB[0:64, :], ofold[other, :], ALU.add).then_inc(o_sum, 1)

            def output_low(g):
                rows = slice(64 * (g % 2), 64 * (g % 2) + 64)
                dve.wait_ge(o_high, g + 1)
                low(ot[rows, g // 2, 1, :], ofold[rows, :], ot[rows, g // 2, 0, :], o_low)

            for g in range(2 * HEADS):
                if g:
                    dve.wait_ge(max_set, 3 * g)
                    dve.wait_ge(exp_set, 4 * g)
                for n, (b, blocks) in enumerate(SORDER):
                    dve.wait_ge(sc_ps, 3 * g + n + 1)
                    for qb in blocks:
                        o, w = SPLACE[qb][1], P * (qb + 1)
                        ps = SB[b][:, o:o + w]
                        if g < HEADS:
                            diag = SB[b][:, o + w - P:o + w]
                            link(nc.vector.tensor_tensor(diag, diag, causal, ALU.add))
                            ins = nc.vector.reduce_max(mx[:, qb:qb + 1], ps, AX.X)
                        else:
                            h = g - HEADS
                            dve.wait_ge(bias_set, h + 1)
                            p = pbuf[:, POFF[qb]:POFF[qb] + w]
                            link(nc.vector.scalar_tensor_tensor(out=p, in0=ps, scalar=DIL_SCALE, in1=bias[:, h % 2, S - w:S],
                                                                op0=ALU.mult, op1=ALU.add))
                            ins = nc.vector.reduce_max(mx[:, qb:qb + 1], p, AX.X)
                    link(ins)
                    nc.vector.tensor_scalar(nm[:, blocks[-1]:blocks[0] + 1], mx[:, blocks[-1]:blocks[0] + 1],
                                            -MLA_SCALE if g < HEADS else -1.0, None, ALU.mult).then_inc(max_set, 1)
                for n, (b, blocks) in enumerate(SORDER):
                    dve.wait_ge(exp_set, 4 * g + (1, 2, 4)[n])
                    if g:
                        dve.wait_ge(p_set, 3 * g)
                    link(nc.vector.reciprocal(rr[:, blocks[-1]:blocks[0] + 1], rs[:, blocks[-1]:blocks[0] + 1]))
                    for qb in blocks:
                        p = pbuf[:, POFF[qb]:POFF[qb] + P * (qb + 1)]
                        ins = nc.vector.tensor_scalar(p, p, rr[:, qb:qb + 1], None, ALU.mult)
                    ins.then_inc(p_set, 1)
                if g:
                    output_sum(g - 1)
                if g >= HEADS - 1 and g % 2 == 1 and g < 2 * HEADS - 1:
                    j = (g - HEADS + 1) // 2
                    dve.wait_ge(qk_high, j + 1)
                    low(qkb[:, j % 2, :, 1, :], dilf[:, 0:2, j, :], qkb[:, j % 2, :, 0, :], qk_low)
                if g + 1 < HEADS:
                    transposed("q", g + 1)
                    transposed("k", g + 1)
                if g % 2 == 0 and g < HEADS:
                    dve.wait_ge(v_high, g // 2 + 1)
                    low(vb[:, :, :, 1, :], vf[:, :, g:g + 2, :], vb[:, :, :, 0, :], v_low)
                if g >= HEADS and g % 2 == 0:
                    transposed("v", g)
                transposed("p0", g)
                transposed("p1", g)
                if g:
                    output_low(g - 1)
                transposed("p2", g)
                unit_event(PRE + (3 * g) // 2)
                if g % 2 == 1:
                    unit_event(PRE + 1 + (3 * g) // 2)
            output_sum(2 * HEADS - 1)
            output_low(2 * HEADS - 1)
            for p in range(PRE + 3 * HEADS, NPROJ):
                unit_event(p)

            for m in range(KD):
                dve.wait_ge(unit_done, RING[("y", m)] + 1)
                dve.wait_ge(gate_set, 2 * m + 2)
                ya, yb = bank[2 * (m % 2)], bank[2 * (m % 2) + 1]
                nc.vector.tensor_tensor(z[:, m, :], ya[:, :], z[:, m, :], ALU.mult).then_inc(mix_read, 1)
                nc.vector.tensor_tensor(z[:, KD + m, :], yb[:, :], z[:, KD + m, :], ALU.mult).then_inc(mix_read, 1)
                dve.wait_ge(mix_read, 2 * m + 2)
                nc.vector.tensor_tensor(z[:, m, :], z[:, m, :], z[:, KD + m, :], ALU.add).then_inc(mix_set, 1)
                if m + 3 < KD:
                    prep(("y", m + 3))
                prep(("out", m))
                dve.wait_ge(mix_high, m + 1)
                low(mixed[:, m, 1, :], z[:, m, :], mixed[:, m, 0, :], mix_low)
            for m in range(3):
                prep(("ff1", m))

            def normalise(buf, t, dev, part=slice(0, D)):
                link(nc.vector.scalar_tensor_tensor(out=buf[:, t, part], in0=buf[:, t, part], scalar=mv[:, t, 0:1],
                                                    in1=lng[:, part], op0=ALU.subtract, op1=ALU.mult))
                if part.start == 0:
                    dve.wait_ge(dev, t + 1)
                    link(nc.vector.reciprocal(rstd[:, t:t + 1], std[:, t:t + 1]))
                return nc.vector.scalar_tensor_tensor(out=buf[:, t, part], in0=buf[:, t, part], scalar=rstd[:, t:t + 1],
                                                      in1=lnb[:, part], op0=ALU.mult, op1=ALU.add)

            def low_h(t):
                for c in range(2):
                    dve.wait_ge(ht_high, 2 * t + c + 1)
                    dst = xt[:, 4 * c:4 * c + 4, :, t * P:(t + 1) * P]
                    low(dst[:, :, 1, :], bank[4 + 2 * (t % 2) + c][:, :].rearrange("p (k n) -> p k n", k=4), dst[:, :, 0, :], ht_low)

            for n in range(2):
                for t in range(NT):
                    half = slice(n * S, (n + 1) * S)
                    dve.wait_ge(out_ps, n * NT + t + 1)
                    if n == 0:
                        dve.wait_ge(x2_in[t], 16)
                    nc.vector.scalar_tensor_tensor(out=hres[:, t, half], in0=xtok[:, t, half], scalar=ALPHA,
                                                   in1=bank[(n * NT + t) % 4][:, :], op0=ALU.mult, op1=ALU.add).then_inc(res_set, 1)
                    dve.wait_ge(res_set, n * NT + t + 1)
                    link(nc.vector.bn_stats(bns[:, t, n, :], hres[:, t, half]))
                    if n == 1:
                        nc.vector.bn_aggr(mv[:, t, :], bns[:, t, :, :].rearrange("p a b -> p (a b)")).then_inc(var_set, 1)
                        if t == 0:
                            dve.wait_ge(ln_in, 32)
                        dve.wait_ge(var_set, t + 1)
                        normalise(hres, t, dev1_set).then_inc(h_set, 1)
                        if 0 < t < NT - 1:
                            low_h(t - 1)
            low_h(NT - 2)
            low_h(NT - 1)

            def squared_low(i, b):
                dve.wait_ge(relu_set, 3 * i + (b + 1))
                nc.vector.tensor_tensor(fsq, relu[:, b, :], relu[:, b, :], ALU.mult).then_inc(fsq_set, 1)
                dve.wait_ge(fsq_set, 3 * i + (b + 1))
                dve.wait_ge(f_high, 3 * i + (b + 1))
                low(ff[:, 3 * i + b, 1, :], fsq, ff[:, 3 * i + b, 0, :], f_low)
                src, high, lo = split_dest(("ff1", b))
                dve.wait_ge(w_high, 3 * i + (POS[("ff1", b)] + 4))
                low(lo, src, high, w_low)

            for b in range(3):
                if b:
                    dve.wait_ge(f_low, b)
                squared_low(0, b)
            with dve.Fori(1, FF1_ROUNDS) as i:
                for b in range(3):
                    dve.wait_ge(f_low, 3 * i + b)
                    squared_low(i, b)
            for b in range(KF - 3 * FF1_ROUNDS):
                dve.wait_ge(f_low, 3 * FF1_ROUNDS + b)
                squared_low(FF1_ROUNDS, b)
            for k in range(KF - LAST):
                if k + 3 < KF - LAST:
                    prep(("ff2", k + 3))
                if k % 3 == 2:
                    prep(("ff2", KF - LAST + k // 3))

            for t in range(NT):
                for n in range(2):
                    half = slice(n * S, (n + 1) * S)
                    dve.wait_ge(ff2_ps, 2 * t + n + 1)
                    dve.wait_ge(h2_in, 16)
                    link(nc.vector.scalar_tensor_tensor(out=h2[:, t, half], in0=h2[:, t, half], scalar=ALPHA,
                                                        in1=bank[2 * t + n][:, :], op0=ALU.mult, op1=ALU.add))
                    link(nc.vector.bn_stats(bns[:, t, n, :], h2[:, t, half]))
                nc.vector.bn_aggr(mv[:, t, :], bns[:, t, :, :].rearrange("p a b -> p (a b)")).then_inc(var2_set, 1)
                dve.wait_ge(ln2_in, 32)
                dve.wait_ge(var2_set, t + 1)
                if t < NT - 1:
                    normalise(h2, t, dev2_set).then_inc(y_set, 1)
                else:
                    for n in range(2):
                        normalise(h2, t, dev2_set, slice(n * S, (n + 1) * S)).then_inc(y_set, 1)

        @block.tensor
        def _(pe):
            PASSES = ((0, 0), (0, 1), (1, 0))

            def product(out_, stationary, moving, first, last):
                for n, (a_, b_) in enumerate(PASSES):
                    ins = nc.tensor.matmul(out_, stationary(a_), moving(b_), start=first and n == 0, stop=last and n == 2)
                return ins

            def ring(u, lo, hi):
                slot = RING[u] % NRING
                return lambda s: (ring_h, ring_l)[s][:, slot, lo:hi]

            pe.wait_ge(small_in, 16)
            for k in range(KD):
                if k >= 6:
                    pe.wait_ge(xt_low, k - 5)
                for t in range(NT):
                    if k % 4 == 0 and t == 0:
                        pe.wait_ge(x_in[k // 4], 16)
                    ins = nc.tensor.transpose(bank[2 + k % 6][:, t * P:(t + 1) * P], xtok[:, t, k * P:(k + 1) * P], ident)
                ins.then_inc(xt_ps, 1)

            def k_step(u, k, acc):
                if k == 0:
                    wait_split(pe, u)
                    if acc >= 2:
                        pe.wait_ge(acc_read, acc - 1)
                ins = product(bank[acc % 2][:, :], ring(u, k * P, (k + 1) * P), lambda s: xt[:, k, s, :], k == 0, k == KD - 1)
                if k == KD - 1:
                    ins.then_inc(unit_done, 1)

            def rotary_step(k, acc):
                if k == 0:
                    wait_split(pe, ("lora", NLORA))
                    pe.wait_ge(acc_read, acc - 1)
                for s in range(2):
                    ins = nc.tensor.matmul(bank[acc % 2][0:2 * ROPE, :], ring(("lora", NLORA), 2 * k * ROPE, 2 * (k + 1) * ROPE)(0),
                                           xt[:, k, s, :], start=k == 0 and s == 0, stop=k == KD - 1 and s == 1)
                if k == KD - 1:
                    ins.then_inc(unit_done, 1)

            def square_sum(c):
                tiles = (range(NQL), range(NQL, NLORA))[c]
                pe.wait_ge(sq_low, tiles[-1] + 1)
                for m in tiles:
                    for s in range(2):
                        ins = nc.tensor.matmul(bank[6 + c][:, :], ones[:, :], sqh[:, m % 4, s, :],
                                               start=(m == tiles[0] and s == 0), stop=(m == tiles[-1] and s == 1))
                ins.then_inc(sum_ps, 1)

            pe.wait_ge(ones_set, 1)
            for m in range(NLORA + 1):
                for k in range(KD):
                    if m == 0:
                        pe.wait_ge(xt_low, k + 1)
                    if m < NLORA:
                        k_step(("lora", m), k, m)
                    else:
                        rotary_step(k, m)
                    if m == NQL and k == 3:
                        square_sum(0)
            filled = [0]

            def fill(steps):
                for _ in range(steps):
                    p, k = divmod(filled[0], KD)
                    k_step(("proj", p), k, NLORA + 1 + p)
                    filled[0] += 1

            fill(3)
            square_sum(1)
            pe.wait_ge(acc_read, NLORA + 1)
            for t in range(NT):
                ins = nc.tensor.transpose(bank[5][:, 2 * t * ROPE:2 * (t + 1) * ROPE], krt[:, t * P:(t + 1) * P],
                                          ident[0:2 * ROPE, 0:2 * ROPE])
            ins.then_inc(krt_ps, 1)

            for i in range(4 * NT):
                t, c, b = (i % 8) // 2, i % 2, 2 + i % 6
                if i == 6:
                    fill(3)
                if i >= 6:
                    pe.wait_ge(qkv_read, i - 5)
                elif b == 5:
                    pe.wait_ge(krot_set, 2)
                elif b >= 6:
                    pe.wait_ge(dev_set, b - 5)
                if i == 0:
                    pe.wait_ge(norm_low, NQL)
                    wait_split(pe, ("uq", NQL - 1))
                if i == 8:
                    pe.wait_ge(norm_low, NLORA)
                    wait_split(pe, ("ukv", NKVL - 1))
                if i < 8:
                    for k in range(NQL):
                        ins = product(bank[b][:, 0:384], lambda s: lora[:, k, s, t * P:(t + 1) * P],
                                      lambda s: uq[k][:, s, c * 384:(c + 1) * 384], k == 0, k == NQL - 1)
                    ins.then_inc(qkv_ps, 1)
                else:
                    for k in range(NKVL):
                        ins = product(bank[b][:, :], lambda s: lora[:, NQL + k, s, t * P:(t + 1) * P],
                                      lambda s: ukv[:, k, s, c * 512:(c + 1) * 512], k == 0, k == NKVL - 1)
                    ins.then_inc(qkv_ps, 1)

            def t_bank(kind, g):
                if TPREV[(kind, g)] is not None:
                    pe.wait_ge(t_low, TPREV[(kind, g)] + 1)
                return TB[TBANK[kind]]

            def transpose_qk(h):
                for kind, src in (("q", qf), ("k", kf)):
                    ps = t_bank(kind, h)
                    for t in range(NT):
                        ins = nc.tensor.transpose(ps[0:QK, t * P:(t + 1) * P], src[:, t, h, :], ident)
                    ins.then_inc(t_ps, 1)

            def transpose_v(g):
                j = (g - HEADS) // 2
                ps = t_bank("v", g)
                pe.wait_ge(acc_read, NLORA + 1 + 3 * j + 3)
                for t in range(NT):
                    ins = nc.tensor.transpose(ps[:, t * P:(t + 1) * P], dilf[:, 2, j, t * P:(t + 1) * P], ident)
                ins.then_inc(t_ps, 1)

            def scores(g):
                if g < HEADS:
                    buf, rows = g % 2, slice(0, QK)
                    pe.wait_ge(t_low, TI[("k", g)] + 1)
                else:
                    j = (g - HEADS) // 2
                    buf, rows = j % 2, slice(64 * (g % 2), 64 * (g % 2) + 64)
                    pe.wait_ge(qk_low, j + 1)
                if g:
                    pe.wait_ge(exp_set, 4 * g)
                for b, blocks in SORDER:
                    for qb in blocks:
                        o, w = SPLACE[qb][1], P * (qb + 1)
                        ins = product(SB[b][:, o:o + w], lambda s: qkb[rows, buf, 0, s, qb * P:(qb + 1) * P],
                                      lambda s: qkb[rows, buf, 1, s, 0:w], True, True)
                    ins.then_inc(sc_ps, 1)

            def transpose_p(g, kind, key_blocks):
                ps = t_bank(kind, g)
                base = KOFF[key_blocks[0]]
                for kb in key_blocks:
                    for qb in range(kb, NT):
                        o = KOFF[kb] - base + (qb - kb) * P
                        ins = nc.tensor.transpose(ps[:, o:o + P], pbuf[:, POFF[qb] + kb * P:POFF[qb] + (kb + 1) * P], ident)
                ins.then_inc(t_ps, 1)

            def weighted_values(g):
                if g:
                    pe.wait_ge(o_sum, g)
                if g < HEADS:
                    pe.wait_ge(v_low, g // 2 + 1)
                for kb in range(NT):
                    pe.wait_ge(t_low, TI[({0: "p0", 1: "p1"}.get(kb, "p2"), g)] + 1)
                    w = S - kb * P
                    for s in range(2):
                        ins = nc.tensor.matmul(OB[:, kb * P:S], vb[:, kb, g % 2, :, :].rearrange("p s d -> p (s d)"),
                                               ptb[:, s, KOFF[kb]:KOFF[kb] + w],
                                               start=(kb == 0 and s == 0), stop=(kb == NT - 1 and s == 1))
                ins.then_inc(pv_ps, 1)

            fill(4)
            pe.wait_ge(q_rot, NT)
            pe.wait_ge(qkv_read, 4 * NT)
            pe.wait_ge(krot_spread, NT)
            transpose_qk(0)
            fill(KD * PRE - filled[0])
            for g in range(2 * HEADS):
                scores(g)
                if g + 1 < HEADS:
                    transpose_qk(g + 1)
                if g >= HEADS and g % 2 == 0:
                    transpose_v(g)
                fill(9)
                pe.wait_ge(p_set, 3 * g + 3)
                transpose_p(g, "p0", (0,))
                transpose_p(g, "p1", (1,))
                fill(2)
                transpose_p(g, "p2", (2, 3))
                fill(1)
                weighted_values(g)
            fill(KD * NPROJ - filled[0])

            for m in range(KD):
                u = ("y", m)
                wait_split(pe, u)
                if m == 0:
                    pe.wait_ge(o_low, 2 * HEADS)
                    pe.wait_ge(acc_read, NLORA + NPROJ)
                if m >= 2:
                    pe.wait_ge(mix_read, 2 * (m - 1))
                for k in range(HEADS):
                    if m == 0 and k == 4:
                        pe.wait_ge(acc_read, NLORA + 1 + NPROJ)
                    ins = product(bank[2 * (m % 2) + k // 4][:, :], ring(u, k * P, (k + 1) * P),
                                  lambda s: ot[:, k, s, :], k % 4 == 0, k % 4 == 3)
                ins.then_inc(unit_done, 1)

            def transpose_h(t):
                pe.wait_ge(h_set, t + 1)
                for c in range(2):
                    if t >= 2:
                        pe.wait_ge(ht_low, 2 * (t - 2) + c + 1)
                    for k in range(4):
                        ins = nc.tensor.transpose(bank[4 + 2 * (t % 2) + c][:, k * P:(k + 1) * P],
                                                  hres[:, t, (4 * c + k) * P:(4 * c + k + 1) * P], ident)
                    ins.then_inc(ht_ps, 1)

            for n in range(2):
                for t in range(NT):
                    i = n * NT + t
                    if i >= 4:
                        pe.wait_ge(res_set, i - 3)
                    else:
                        pe.wait_ge(mix_read, 2 * KD if i >= 2 else 2 * KD - 2)
                    for k in range(KD):
                        if i == 0:
                            wait_split(pe, ("out", k))
                            pe.wait_ge(mix_low, k + 1)
                        ins = product(bank[i % 4][:, :], lambda s: mixed[:, k, s, t * P:(t + 1) * P],
                                      lambda s: wout[n][:, k, s, :], k == 0, k == KD - 1)
                        if k == 1 and n == 1 and t >= 2:
                            transpose_h(t - 2)
                    ins.then_inc(out_ps, 1)

            def hidden(i, b, tokens=slice(0, S)):
                pe.wait_ge(w_low, 3 * i + LOW_COUNT[("ff1", b)])
                for k in range(KD):
                    ins = product(bank[b][:, tokens], ring(("ff1", b), k * P, (k + 1) * P), lambda s: xt[:, k, s, tokens],
                                  k == 0, k == KD - 1)
                return ins

            early, late = slice(0, S // 2), slice(S // 2, S)
            pe.wait_ge(ht_low, NT)
            pe.wait_ge(res_set, NT + 1)
            hidden(0, 0, early)
            transpose_h(NT - 2)
            pe.wait_ge(res_set, NT + 2)
            hidden(0, 1, early)
            pe.wait_ge(res_set, NT + 3)
            transpose_h(NT - 1)
            hidden(0, 2, early)
            pe.wait_ge(ht_low, 2 * NT)
            for b in range(3):
                hidden(0, b, late).then_inc(unit_done, 1)
            with pe.Fori(1, FF1_ROUNDS) as i:
                for b in range(3):
                    pe.wait_ge(relu_set, 3 * i + (b - 2))
                    hidden(i, b).then_inc(unit_done, 1)
            for b in range(KF - 3 * FF1_ROUNDS):
                pe.wait_ge(relu_set, 3 * FF1_ROUNDS + (b - 2))
                hidden(FF1_ROUNDS, b).then_inc(unit_done, 1)

            for k in range(KF - LAST):
                u = ("ff2", k)
                wait_split(pe, u)
                pe.wait_ge(f_low, k + 1)
                for t in (2, 3, 0, 1):
                    if k == 0 and t == 0:
                        pe.wait_ge(relu_set, KF)
                    for a_, b_ in PASSES:
                        for n in range(2):
                            ins = nc.tensor.matmul(bank[2 * t + n][:, :], ff[:, k, a_, t * P:(t + 1) * P],
                                                   ring(u, n * S, (n + 1) * S)(b_), start=(k == 0 and a_ == 0 and b_ == 0), stop=False)
                ins.then_inc(unit_done, 1)
            for t in range(NT):
                for n in range(2):
                    for j in range(LAST):
                        k = KF - LAST + j
                        if t == 0 and n == 0:
                            wait_split(pe, ("ff2", k))
                            pe.wait_ge(f_low, k + 1)
                        w2 = lambda s: ff[:, 2 * j + s, n, :]
                        ins = product(bank[2 * t + n][:, :], lambda s: ff[:, k, s, t * P:(t + 1) * P], w2, False, j == LAST - 1)
                    ins.then_inc(ff2_ps, 1)


INPUTS = ["x", "w_in", "b_gate", "g_q_a", "w_uq", "g_kv_a", "w_ukv", "w_o_mla", "w_o_dil", "w_out",
          "ln1_g", "ln1_b", "w_ff1", "w_ff2", "ln2_g", "ln2_b"]


def kernel(**inputs):
    import concourse.bacc as bacc
    from concourse.bass_utils import run_bass_kernel_spmd as run

    nc = bacc.Bacc("TRN2", target_bir_lowering=False, num_devices=1)
    arrays, aps = {}, {}
    for name in INPUTS:
        arrays[f"in_{name}"] = np.ascontiguousarray(inputs[name])
    arrays["in_const"] = constants()
    for name, v in arrays.items():
        aps[name[3:]] = nc.dram_tensor(name, v.shape, F32, kind="ExternalInput").ap()
    y = nc.dram_tensor("out_y", (1, S, D), F32, kind="ExternalOutput").ap()
    layer_kernel(nc, aps, y)
    return run(nc, [arrays], core_ids=[0]).results[0]["out_y"]
```
